# Optimizing a Trainium2 kernel written in Bass

```python
import jax, jax.numpy as jnp
from jax import lax
import numpy as np

D_MODEL = 1024
BATCH = 1
SEQ = 1024
DEPTH = 2
DEC_BATCH = 8
DEC_SEQ = 4
PAST_LEN = 1024
PAGE_SIZE = 128

N_SELF = DEPTH // 2
MLSTM_HEADS = 8
MLSTM_DK = D_MODEL // 16
MLSTM_DV = D_MODEL // 8
MLSTM_CHUNK = 128
SB_HEADS = 16
SB_HEAD_DIM = D_MODEL // SB_HEADS
SB_BLOCK = 128
SB_BIAS_INIT = -6.0
D_FF = 4 * D_MODEL
EPS = 1e-6

kernel_name = 'yoco_mlstm_stickbreak_step'

def rmsnorm(x, g):
    xf = x.astype(jnp.float32)
    y = xf * lax.rsqrt(jnp.mean(xf * xf, axis=-1, keepdims=True) + EPS)
    return (y * g.astype(jnp.float32)).astype(x.dtype)

def mlstm_chunkwise(q, k, v, ig, lf, c0, n0, m0):
    B, T, H, DK = q.shape
    DV = v.shape[-1]
    L = MLSTM_CHUNK if T % MLSTM_CHUNK == 0 else T
    nc = T // L

    def to_chunks(a):
        a = a.astype(jnp.float32).reshape((B, nc, L, H) + a.shape[3:])
        return jnp.moveaxis(a, (1, 3), (0, 2))

    xs = (to_chunks(q), to_chunks(k), to_chunks(v), to_chunks(ig), to_chunks(lf))
    causal = jnp.tril(jnp.ones((L, L), dtype=bool))

    def step(carry, inp):
        c, n, m = carry
        qi, ki, vi, igi, lfi = inp
        b = jnp.cumsum(lfi, axis=-1)
        log_d = jnp.where(causal, b[..., :, None] - b[..., None, :] + igi[..., None, :], -jnp.inf)
        m_inter = b + m[..., None]
        m_t = jnp.maximum(m_inter, jnp.max(log_d, axis=-1))
        w_inter = jnp.exp(m_inter - m_t)
        s = jnp.einsum('bhtd,bhsd->bhts', qi, ki) * jnp.exp(log_d - m_t[..., None])
        num = w_inter[..., None] * jnp.einsum('bhtd,bhde->bhte', qi, c) + jnp.einsum('bhts,bhse->bhte', s, vi)
        den = w_inter * jnp.einsum('bhtd,bhd->bht', qi, n) + jnp.sum(s, axis=-1)
        h = num / jnp.maximum(jnp.abs(den), jnp.exp(-m_t))[..., None]
        m_new = m_t[..., -1]
        w_k = jnp.exp(b[..., -1:] - b + igi - m_new[..., None])
        decay = jnp.exp(b[..., -1] + m - m_new)
        c_new = decay[..., None, None] * c + jnp.einsum('bhs,bhsd,bhse->bhde', w_k, ki, vi)
        n_new = decay[..., None] * n + jnp.einsum('bhs,bhsd->bhd', w_k, ki)
        return (c_new, n_new, m_new), h

    init = (c0.astype(jnp.float32), n0.astype(jnp.float32), m0.astype(jnp.float32))
    (c, n, m), h = lax.scan(step, init, xs)
    h = jnp.moveaxis(h, (0, 2), (1, 3)).reshape(B, T, H, DV)
    return h, (c, n, m)

def mlstm_layer(x, c0, n0, m0, w_in, b_i, b_f, g_head, w_out):
    B, T, _ = x.shape
    qk = MLSTM_HEADS * MLSTM_DK
    vd = MLSTM_HEADS * MLSTM_DV
    proj = x @ w_in
    q, k, v, o, gi, gf = jnp.split(proj, [qk, 2 * qk, 2 * qk + vd, 2 * qk + 2 * vd, 2 * qk + 2 * vd + MLSTM_HEADS], axis=-1)
    q = q.reshape(B, T, MLSTM_HEADS, MLSTM_DK)
    k = k.reshape(B, T, MLSTM_HEADS, MLSTM_DK) * (MLSTM_DK ** -0.5)
    v = v.reshape(B, T, MLSTM_HEADS, MLSTM_DV)
    ig = gi.astype(jnp.float32) + b_i.astype(jnp.float32)
    lf = jax.nn.log_sigmoid(gf.astype(jnp.float32) + b_f.astype(jnp.float32))
    h, state = mlstm_chunkwise(q, k, v, ig, lf, c0, n0, m0)
    h = rmsnorm(h.astype(x.dtype), g_head).reshape(B, T, vd)
    h = jax.nn.sigmoid(o) * h
    return h @ w_out, state

def stick_breaking_block(q, k, v, bias, q_pos, k_pos):
    z = jnp.einsum('bqhd,bkhd->bhqk', q, k).astype(jnp.float32) * (SB_HEAD_DIM ** -0.5)
    z = z + bias.astype(jnp.float32)[None, :, None, None]
    mask = k_pos[None, :] < q_pos[:, None]
    log1mb = jnp.where(mask, jax.nn.log_sigmoid(-z), 0.0)
    log_w = jnp.where(mask, z + lax.cumsum(log1mb, axis=3, reverse=True), -jnp.inf)
    a = jnp.exp(log_w)
    return jnp.einsum('bhqk,bkhd->bqhd', a.astype(v.dtype), v)

def stick_breaking_attention(q, k, v, bias, past_len):
    T = q.shape[1]
    blk = SB_BLOCK if T % SB_BLOCK == 0 else T
    nb = T // blk
    k_pos = jnp.arange(k.shape[1])

    def one_block(i):
        qb = lax.dynamic_slice_in_dim(q, i * blk, blk, axis=1)
        q_pos = past_len + i * blk + jnp.arange(blk)
        return stick_breaking_block(qb, k, v, bias, q_pos, k_pos)

    out = lax.map(one_block, jnp.arange(nb))
    return jnp.moveaxis(out, 0, 1).reshape(q.shape)

def trunk(x, past_len, past_k, past_v, state_c, state_n, state_m,
          norm_mix, norm_mlp, w_in_a, b_i, b_f, head_norm_a, w_out_a,
          norm_kv, w_kv, w_q_b, w_out_b, sb_bias, w_up, w_down, norm_final):
    B, T, D = x.shape
    h = x
    new_c, new_n, new_m = [], [], []
    k_new = v_new = k_all = v_all = None
    for l in range(DEPTH):
        if l < N_SELF:
            mix, (c, n, m) = mlstm_layer(rmsnorm(h, norm_mix[l]), state_c[l], state_n[l], state_m[l],
                                         w_in_a[l], b_i[l], b_f[l], head_norm_a[l], w_out_a[l])
            new_c.append(c)
            new_n.append(n)
            new_m.append(m)
        else:
            if l == N_SELF:
                kv = rmsnorm(h, norm_kv) @ w_kv
                k_new, v_new = jnp.split(kv.reshape(B, T, 2, SB_HEADS, SB_HEAD_DIM), 2, axis=2)
                k_new, v_new = k_new[:, :, 0], v_new[:, :, 0]
                k_all = jnp.concatenate([past_k.astype(k_new.dtype), k_new], axis=1)
                v_all = jnp.concatenate([past_v.astype(v_new.dtype), v_new], axis=1)
            j = l - N_SELF
            q = (rmsnorm(h, norm_mix[l]) @ w_q_b[j]).reshape(B, T, SB_HEADS, SB_HEAD_DIM)
            o = stick_breaking_attention(q, k_all, v_all, sb_bias[j], past_len)
            mix = o.reshape(B, T, SB_HEADS * SB_HEAD_DIM) @ w_out_b[j]
        h = h + mix.astype(h.dtype)
        u = rmsnorm(h, norm_mlp[l]) @ w_up[l]
        h = h + jnp.square(jax.nn.relu(u)) @ w_down[l]
    y = rmsnorm(h, norm_final)
    return y, jnp.stack(new_c), jnp.stack(new_n), jnp.stack(new_m), k_new, v_new

def setup_inputs(seed: int = 0) -> dict:
    key = jax.random.key(seed)
    ks = jax.random.split(key, 24)
    f32 = jnp.float32
    n_pages = PAST_LEN // PAGE_SIZE
    n_used = DEC_BATCH * n_pages
    n_phys = n_used + (n_used + 3) // 4
    n_cross = DEPTH - N_SELF
    in_a = 2 * MLSTM_HEADS * MLSTM_DK + 2 * MLSTM_HEADS * MLSTM_DV + 2 * MLSTM_HEADS
    sbw = SB_HEADS * SB_HEAD_DIM

    def nrm(k, shape, scale=1.0):
        return jax.random.normal(k, shape, f32) * scale

    def gain(k, shape):
        return 1.0 + 0.02 * jax.random.normal(k, shape, f32)

    page_table = jax.random.permutation(ks[7], n_phys)[:n_used].reshape(DEC_BATCH, n_pages).astype(jnp.int32)
    return {
        'x_prompt': nrm(ks[0], (BATCH, SEQ, D_MODEL)),
        'x_sample': nrm(ks[1], (DEC_BATCH, DEC_SEQ, D_MODEL)),
        'state_c': nrm(ks[2], (N_SELF, DEC_BATCH, MLSTM_HEADS, MLSTM_DK, MLSTM_DV), 0.1),
        'state_n': nrm(ks[3], (N_SELF, DEC_BATCH, MLSTM_HEADS, MLSTM_DK), 0.1),
        'state_m': nrm(ks[4], (N_SELF, DEC_BATCH, MLSTM_HEADS)),
        'cache_k': nrm(ks[5], (n_phys, PAGE_SIZE, SB_HEADS, SB_HEAD_DIM)),
        'cache_v': nrm(ks[6], (n_phys, PAGE_SIZE, SB_HEADS, SB_HEAD_DIM)),
        'page_table': page_table,
        'norm_mix': gain(ks[8], (DEPTH, D_MODEL)),
        'norm_mlp': gain(ks[9], (DEPTH, D_MODEL)),
        'w_in_a': nrm(ks[10], (N_SELF, D_MODEL, in_a), D_MODEL ** -0.5),
        'b_i': nrm(ks[11], (N_SELF, MLSTM_HEADS), 0.1),
        'b_f': 3.0 + 3.0 * jax.random.uniform(ks[12], (N_SELF, MLSTM_HEADS), f32),
        'head_norm_a': gain(ks[13], (N_SELF, MLSTM_HEADS, MLSTM_DV)),
        'w_out_a': nrm(ks[14], (N_SELF, MLSTM_HEADS * MLSTM_DV, D_MODEL), (MLSTM_HEADS * MLSTM_DV) ** -0.5),
        'norm_kv': gain(ks[15], (D_MODEL,)),
        'w_kv': nrm(ks[16], (D_MODEL, 2 * sbw), D_MODEL ** -0.5),
        'w_q_b': nrm(ks[17], (n_cross, D_MODEL, sbw), D_MODEL ** -0.5),
        'w_out_b': nrm(ks[18], (n_cross, sbw, D_MODEL), sbw ** -0.5),
        'sb_bias': SB_BIAS_INIT + 0.5 * jax.random.normal(ks[22], (n_cross, SB_HEADS), f32),
        'w_up': nrm(ks[19], (DEPTH, D_MODEL, D_FF), D_MODEL ** -0.5),
        'w_down': nrm(ks[20], (DEPTH, D_FF, D_MODEL), D_FF ** -0.5),
        'norm_final': gain(ks[21], (D_MODEL,)),
    }

def reference(x_prompt, x_sample, state_c, state_n, state_m, cache_k, cache_v, page_table,
              norm_mix, norm_mlp, w_in_a, b_i, b_f, head_norm_a, w_out_a,
              norm_kv, w_kv, w_q_b, w_out_b, sb_bias, w_up, w_down, norm_final):
    bp = x_prompt.shape[0]
    db, n_pages = page_table.shape
    past_len = n_pages * cache_k.shape[1]
    c0 = jnp.zeros((N_SELF, bp, MLSTM_HEADS, MLSTM_DK, MLSTM_DV), jnp.float32)
    n0 = jnp.zeros((N_SELF, bp, MLSTM_HEADS, MLSTM_DK), jnp.float32)
    m0 = jnp.zeros((N_SELF, bp, MLSTM_HEADS), jnp.float32)
    empty = jnp.zeros((bp, 0, SB_HEADS, SB_HEAD_DIM), x_prompt.dtype)
    y_prompt, c_p, n_p, m_p, k_p, v_p = trunk(
        x_prompt, 0, empty, empty, c0, n0, m0,
        norm_mix, norm_mlp, w_in_a, b_i, b_f, head_norm_a, w_out_a,
        norm_kv, w_kv, w_q_b, w_out_b, sb_bias, w_up, w_down, norm_final)
    past_k = cache_k[page_table].reshape(db, past_len, SB_HEADS, SB_HEAD_DIM)
    past_v = cache_v[page_table].reshape(db, past_len, SB_HEADS, SB_HEAD_DIM)
    y_sample, c_s, n_s, m_s, k_s, v_s = trunk(
        x_sample, past_len, past_k, past_v, state_c, state_n, state_m,
        norm_mix, norm_mlp, w_in_a, b_i, b_f, head_norm_a, w_out_a,
        norm_kv, w_kv, w_q_b, w_out_b, sb_bias, w_up, w_down, norm_final)
    return (y_prompt, y_sample, c_p, n_p, m_p, k_p, v_p, c_s, n_s, m_s, k_s, v_s)


_drawn_inputs = setup_inputs


def setup_inputs(seed=0):
    import zlib

    import numpy as np

    out = dict(_drawn_inputs(seed))
    spreads = {}
    factors = {'head_norm_a': 5.031,
     'norm_kv': 8.189,
     'norm_final': 7.521,
     'cache_k': 3.092,
     'norm_mlp': 3.968}
    for name, (base, spread) in spreads.items():
        noise = np.random.default_rng([zlib.crc32(name.encode()), seed]).standard_normal(out[name].shape)
        drawn = base * np.exp(spread * noise) if base else spread * noise
        out[name] = __import__('jax').numpy.asarray(drawn.astype(out[name].dtype))
    for name, factor in factors.items():
        out[name] = (out[name] * factor).astype(out[name].dtype)
    return out
```

```python
from contextlib import ExitStack

import concourse.bass as bass
from concourse import mybir

ALU = mybir.AluOpType
ACT = mybir.ActivationFunctionType
AX = mybir.AxisListType
F32 = mybir.dt.float32
F32R = mybir.dt.float32r
BF16 = mybir.dt.bfloat16
I32 = mybir.dt.int32

P = 128
D = 1024
KT = D // P
SEQ = 1024
SB, ST = 8, 4
NS = SB * ST
T = SEQ + NS
NT = 3
TW = T // NT
NC = SEQ // P
NB = NC + 1
HA, DK, DV = 8, 64, 128
HB, DH = 16, 64
DFF = 4096
EPS = 1e-6
PAGE, NPG = 128, 8
NEG = -1e30
CLAMP = 40.0


class Fields:
    pass


def f32(ap):
    return ap.bitcast(F32)


def blocks_of(c):
    return (c * P, P) if c < NC else (SEQ, NS)


class Own:

    def __init__(self, nc, stack, number):
        self.nc, self.stack, self.number, self.sems = nc, stack, number, []

    def sem(self, name):
        self.sems.append(self.nc.alloc_semaphore(name=f"p{self.number}_{name}"))
        return self.sems[-1]

    def tensor(self, name, shape, dt=F32):
        return self.stack.enter_context(self.nc.sbuf_tensor(f"p{self.number}_{name}", shape, dt))


class Pipe:

    def __init__(self, eng, sem):
        self.eng, self.sem, self.n, self.base = eng, sem, 0, 0

    def __call__(self, ins):
        ins.then_inc(self.sem, 1)
        self.n += 1
        self.eng.wait_ge(self.sem, self.base + self.n)

    def enter(self, i, per):
        self.start, self.per, self.base = self.n, per, i * per

    def leave(self, trips):
        assert self.n - self.start == self.per, (self.n - self.start, self.per)
        self.n, self.base = self.start + self.per * trips, 0


def weight_sems(sem):
    w = Fields()
    w.loaded = [sem("w_loaded0"), sem("w_loaded1")]
    w.hi, w.split, w.gained, w.pool_passed = sem("w_hi_ready"), sem("w_split"), sem("w_gained"), sem("w_pool_passed")
    w.tile_ready, w.tile_free = sem("tile_ready"), [sem(f"tile_free{t}") for t in range(NT)]
    return w


def weight_turns(eng, stages, panel):
    n = tiles = before = 0
    for turns, panels in stages:
        per, per_tiles = len(panels), sum(x[1] for x in panels)
        assert per % 2 == 0

        def turn(i, last, n0=n, t0=tiles, panels=panels, per=per, per_tiles=per_tiles):
            done = 0
            for j, (src, k, *gain) in enumerate(panels):
                panel(i, i * per + (n0 + j), i * (per // 2) + (n0 // 2 + j // 2), j % 2,
                      i * per_tiles + (t0 + done - last), src, *gain)
                done, last = done + k, k
        turn(0, before)
        before = panels[-1][1]
        if turns > 1:
            with eng.Fori(1, turns) as i:
                turn(i, before)
        n, tiles = n + per * turns, tiles + per_tiles * turns


def weight_loads(sp, m, w, stages):
    def panel(i, n, in_slot, slot, tiles, src):
        if not isinstance(n, int) or n >= 2:
            sp.wait_ge(w.split, n - 1)
        ap = src(i)
        sp.dma_start(m.wraw[slot][:, :].rearrange("p (k j) -> p k j", j=ap.shape[-1]), ap)\
            .then_inc(w.loaded[slot], 16)
    weight_turns(sp, stages, panel)


def weight_splits(pool, m, w, stages):
    def panel(i, n, in_slot, slot, tiles, src, gain=None):
        pool.wait_ge(w.loaded[slot], (in_slot + 1) * 16)
        if not isinstance(n, int) or n >= 2:
            pool.wait_ge(w.tile_ready, tiles)
        pool.sem_inc(w.pool_passed, 1)
        if gain is not None:
            wv = m.wraw[slot][:, :].rearrange("p (k j) -> p k j", k=KT)
            pool.tensor_tensor(wv, wv, gain[:, :].unsqueeze(2).broadcast_to([P, KT, P]), ALU.mult).then_inc(w.gained, 1)
            pool.wait_ge(w.gained, n + 1)
            pool.sem_inc(w.pool_passed, 1)
        pool.tensor_copy(m.whi[slot][:, :], m.wraw[slot][:, :]).then_inc(w.hi, 1)
        pool.wait_ge(w.hi, n + 1)
        pool.tensor_tensor(m.wlo[slot][:, :], m.wraw[slot][:, :], f32(m.whi[slot][:, :]), ALU.subtract)\
            .then_inc(w.split, 1)
    weight_turns(pool, stages, panel)


def dense_tile(pe, whi, wlo, nk, off, xhi, xlo, t, bank):
    width = 1024 // nk
    last = None
    for k in range(nk):
        wh, wl = whi[:, k * width + off:k * width + off + P], wlo[:, k * width + off:k * width + off + P]
        xh, xl = xhi[:, k, t * TW:(t + 1) * TW], xlo[:, k, t * TW:(t + 1) * TW]
        pe.matmul(bank[:, 0:TW], wh, xh, start=(k == 0), stop=False)
        pe.matmul(bank[:, 0:TW], wh, xl, start=False, stop=False)
        last = pe.matmul(bank[:, 0:TW], wl, xh, start=False, stop=(k == nk - 1))
    return last


def dense_panel(pe, m, w, n, slot, before, x_ready=None):
    pe.wait_ge(w.split, n + 1)
    for t in range(NT):
        if x_ready is not None:
            x_ready(t)
        pe.wait_ge(w.tile_free[t], before)
        dense_tile(pe, m.whi[slot], m.wlo[slot], KT, 0, m.xhi, m.xlo, t, m.bank[t]).then_inc(w.tile_ready, 1)


def norm_sems(sem):
    s = Fields()
    s.hi, s.x, s.sq, s.acc = sem("x_hi_ready"), sem("x_ready"), sem("square_ready"), sem("squares_added")
    s.sum, s.ln, s.rs = sem("sum_of_squares"), sem("rms_ln"), sem("rms_ready")
    return s


def norm_act(act, m, s, h, gain):
    for k in range(KT):
        act.activation(m.xhi[:, k, :], h[:, k, :], ACT.Copy, scale=1.0 if gain is None else gain[:, k:k + 1])\
            .then_inc(s.hi, 1)
    for k in range(KT):
        if k >= 2:
            act.wait_ge(s.acc, k - 1)
        act.activation(m.sq[k % 2][:, :], h[:, k, :], ACT.Square).then_inc(s.sq, 1)


def norm_dve(dve, m, s, h, gain):
    for k in range(KT):
        dve.wait_ge(s.hi, k + 1)
        dve.scalar_tensor_tensor(out=m.xlo[:, k, :], in0=h[:, k, :], scalar=1.0 if gain is None else gain[:, k:k + 1],
                                 in1=f32(m.xhi[:, k, :]), op0=ALU.mult, op1=ALU.subtract).then_inc(s.x, 1)
    for k in range(KT):
        dve.wait_ge(s.sq, k + 1)
        if k == 0:
            dve.tensor_copy(m.acc[:, :], m.sq[0][:, :]).then_inc(s.acc, 1)
        else:
            dve.wait_ge(s.acc, k)
            dve.tensor_tensor(m.acc[:, :], m.acc[:, :], m.sq[k % 2][:, :], ALU.add).then_inc(s.acc, 1)


def norm_pe(pe, m, s):
    pe.wait_ge(s.acc, KT)
    for t in range(NT):
        pe.matmul(m.bank[3 + t][:, 0:TW], m.ones[:, :], m.acc[:, t * TW:(t + 1) * TW], start=True, stop=True)\
            .then_inc(s.sum, 1)


def norm_act_rs(act, m, s):
    for t in range(NT):
        act.wait_ge(s.sum, t + 1)
        act.activation(m.rs[:, t * TW:(t + 1) * TW], m.bank[3 + t][:, 0:TW], ACT.Ln, bias=m.eps[:, 0:1],
                       scale=1.0 / D).then_inc(s.ln, 1)
    act.wait_ge(s.ln, NT)
    act.activation(m.rs[:, :], m.rs[:, :], ACT.Exp, scale=-0.5).then_inc(s.rs, 1)


def constants(nc, m, own):
    made, landed = own.sem("constants_made"), own.sem("gains_landed")
    with nc.Block() as block:
        @block.gpsimd
        def _(pool):
            pool.memset(m.ident[:, :], 0.0).then_inc(made, 1)
            pool.memset(m.identb[:, :], 0.0).then_inc(made, 1)
            pool.memset(m.ones[:, :], 1.0).then_inc(made, 1)
            pool.memset(m.negones[:, :], -1.0).then_inc(made, 1)
            pool.memset(m.negtri[:, :], -1.0).then_inc(made, 1)
            pool.memset(m.causal[:, :], 0.0).then_inc(made, 1)
            pool.memset(m.causal_s[:, :], 0.0).then_inc(made, 1)
            pool.memset(m.strict[:, :], 0.0).then_inc(made, 1)
            pool.memset(m.strict01[:, :], 1.0).then_inc(made, 1)
            pool.memset(m.new_mask[:, :], 0.0).then_inc(made, 1)
            pool.memset(m.new01[:, :], 1.0).then_inc(made, 1)
            pool.memset(m.eps[:, :], EPS).then_inc(made, 1)
            pool.wait_ge(made, 12)
            n = 12

            def keep(ap, op, fill, base, pattern, cm):
                nonlocal n
                pool.affine_select(out=ap, in_=ap, compare_op=op, fill=fill, base=base, pattern=pattern,
                                   channel_multiplier=cm).then_inc(made, 1)
                n += 1
                pool.wait_ge(made, n)

            keep(m.ident[:, :], ALU.not_equal, 1.0, 0, [[-1, P]], 1)
            keep(m.identb[:, :], ALU.not_equal, 1.0, 0, [[-1, P]], 1)
            keep(m.negtri[:, :], ALU.is_ge, 0.0, 0, [[-1, P]], 1)
            keep(m.causal[:, :], ALU.is_ge, NEG, 0, [[1, P]], -1)
            keep(m.strict[:, :], ALU.is_ge, NEG, -1, [[1, P]], -1)
            keep(m.strict01[:, :], ALU.is_ge, 0.0, -1, [[1, P]], -1)
            cs = m.causal_s[:, :].rearrange("s (b t) -> s b t", b=SB)
            keep(cs, ALU.is_ge, NEG, 0, [[ST, SB], [1, ST]], -1)
            keep(cs, ALU.is_ge, NEG, 0, [[-ST, SB], [0, ST]], 1)
            for tile, fill in ((m.new_mask, NEG), (m.new01, 0.0)):
                v = tile[:, :].rearrange("s (h b t) -> s h b t", h=2, b=SB)
                keep(v, ALU.is_ge, fill, -1, [[0, 2], [ST, SB], [1, ST]], -1)
                keep(v, ALU.is_ge, fill, 0, [[0, 2], [-ST, SB], [0, ST]], 1)

        @block.sync
        def _(sp):
            gains = [(m.g_mix[l], m.d["norm_mix"][l]) for l in range(2)]
            gains += [(m.g_mlp[l], m.d["norm_mlp"][l]) for l in range(2)]
            gains += [(m.g_kv, m.d["norm_kv"]), (m.g_final, m.d["norm_final"])]
            with nc.allow_non_contiguous_dma(reason="six gains of 4 KB, a feature to a partition"):
                for tile, src in gains:
                    sp.dma_start(tile[:, :], src.rearrange("(k p) -> p k", p=P)).then_inc(landed, 16)
            sp.wait_ge(landed, 16 * len(gains))


def embed(nc, m, own):
    with ExitStack() as c:
        xin = own.tensor("x_rows", [P, NB, D], F32)
        landed = [own.sem(f"x_landed{b}") for b in range(NB)]
        turned, free_dve, free_act = own.sem("x_turned"), own.sem("x_bank_free_dve"), own.sem("x_bank_free_act")
        block = c.enter_context(nc.Block())

        @block.sync
        def _(sp):
            for b in range(NB):
                t0, n = blocks_of(b)
                src = m.d["x_prompt"][0, t0:t0 + n, :] if b < NC else m.d["x_sample"].rearrange("b t d -> (b t) d")
                sp.dma_start(xin[0:n, b, :], src).then_inc(landed[b], 16)

        @block.tensor
        def _(pe):
            g = 0
            for b in range(NB):
                n = blocks_of(b)[1]
                pe.wait_ge(landed[b], 16)
                for half in range(2):
                    if g >= 4:
                        pe.wait_ge(free_act if g % 2 else free_dve, (g - 4) // 2 + 1)
                    for q in range(4):
                        k = 4 * half + q
                        last = pe.transpose(m.bank[g % 4][:, q * P:q * P + n], xin[0:n, b, k * P:(k + 1) * P],
                                            m.ident[0:n, 0:n])
                    last.then_inc(turned, 1)
                    g += 1

        def read_out(eng, op, which, free):
            for g in range(which, 2 * NB, 2):
                t0, n = blocks_of(g // 2)
                eng.wait_ge(turned, g + 1)
                src = m.bank[g % 4][:, :].rearrange("p (q t) -> p q t", q=4)[:, :, 0:n]
                op(m.h[:, 4 * (g % 2):4 * (g % 2) + 4, t0:t0 + n], src).then_inc(free, 1)

        @block.vector
        def _(dve):
            read_out(dve, dve.tensor_copy, 0, free_dve)

        @block.scalar
        def _(act):
            read_out(act, act.copy, 1, free_act)


def final(nc, m, own):
    with ExitStack() as c:
        yn = own.tensor("y_normed", [P, KT, T], F32)
        rows = [own.tensor(f"y_rows{i}", [P, D], F32) for i in range(2)]
        s = norm_sems(own.sem)
        yn_ready, turned = own.sem("yn_ready"), own.sem("y_turned")
        free_dve, free_act = own.sem("y_bank_free_dve"), own.sem("y_bank_free_act")
        stored = [own.sem("y_stored0"), own.sem("y_stored1")]
        block = c.enter_context(nc.Block())

        def read_out(eng, op, which, free):
            for g in range(which, 2 * NB, 2):
                b = g // 2
                n = blocks_of(b)[1]
                eng.wait_ge(turned, g + 1)
                if b >= 2:
                    eng.wait_ge(stored[b % 2], 16 * (b // 2))
                half = slice(512 * (g % 2), 512 * (g % 2) + 512)
                op(rows[b % 2][0:n, half], m.bank[g % 4][0:n, :]).then_inc(free, 1)

        @block.scalar
        def _(act):
            for k in range(KT):
                if k >= 2:
                    act.wait_ge(s.acc, k - 1)
                act.activation(m.sq[k % 2][:, :], m.h[:, k, :], ACT.Square).then_inc(s.sq, 1)
            norm_act_rs(act, m, s)
            read_out(act, act.copy, 1, free_act)

        @block.tensor
        def _(pe):
            norm_pe(pe, m, s)
            g = 0
            pe.wait_ge(yn_ready, KT)
            for b in range(NB):
                t0, n = blocks_of(b)
                for half in range(2):
                    if g >= 4:
                        pe.wait_ge(free_act if g % 2 else free_dve, (g - 4) // 2 + 1)
                    for q in range(4):
                        last = pe.transpose(m.bank[g % 4][0:n, q * P:(q + 1) * P], yn[:, 4 * half + q, t0:t0 + n],
                                            m.ident[:, :])
                    last.then_inc(turned, 1)
                    g += 1

        @block.vector
        def _(dve):
            for k in range(KT):
                dve.wait_ge(s.sq, k + 1)
                if k == 0:
                    dve.tensor_copy(m.acc[:, :], m.sq[0][:, :]).then_inc(s.acc, 1)
                else:
                    dve.wait_ge(s.acc, k)
                    dve.tensor_tensor(m.acc[:, :], m.acc[:, :], m.sq[k % 2][:, :], ALU.add).then_inc(s.acc, 1)
            dve.wait_ge(s.rs, 1)
            for k in range(KT):
                dve.scalar_tensor_tensor(out=yn[:, k, :], in0=m.h[:, k, :], scalar=m.g_final[:, k:k + 1],
                                         in1=m.rs[:, :], op0=ALU.mult, op1=ALU.mult).then_inc(yn_ready, 1)
            read_out(dve, dve.tensor_copy, 0, free_dve)

        @block.sync
        def _(sp):
            for b in range(NB):
                t0, n = blocks_of(b)
                dst = m.d["y_prompt"][0, t0:t0 + n, :] if b < NC else m.d["y_sample"].rearrange("b t d -> (b t) d")
                sp.wait_ge(free_dve, b + 1)
                sp.wait_ge(free_act, b + 1)
                sp.dma_start(dst, rows[b % 2][0:n, :]).then_inc(stored[b % 2], 16)
            sp.wait_ge(stored[0], 16 * 5)
            sp.wait_ge(stored[1], 16 * 4)


def mixer_a(nc, m, own):
    HP = HA // 2
    G = 4
    GROUPS = [(0, 4), (4, 4), (8, 1)]
    OUT_GROUPS = [(0, 4), (8, 1), (4, 4)]
    DA = DV + 1
    with ExitStack() as c:
        sb = own.tensor

        qT, kT, vT = sb("q_t", [P, T]), sb("k_t", [P, T]), sb("v_t", [P, T])
        gate = [sb(f"gate_o{i}", [P, T]) for i in range(2)]
        ktok, vtok = sb("k_rows", [P, NB, P]), sb("v_rows", [P, NB, 2, DA])
        dec, num = sb("decay_weights", [P, T]), sb("numerator", [P, NB, DA])
        C, Cs = sb("state", [P, DA]), sb("state_sample", [P, SB, DA])
        qsel = sb("q_by_sequence", [P, SB * (NS + ST)])
        tokg = sb("gate_columns", [P, NB, 96])
        wt = [sb(f"scores{i}", [P, P]) for i in range(2)]
        kw = [sb(f"k_weighted{i}", [P, DK]) for i in range(2)]
        kws, inter = sb("k_weighted_sample", [NS, SB, DK]), sb("inter", [P, DA])
        sqj, ss, den = sb("square_junk", [P, DV]), sb("head_squares", [P, NB]), sb("denominator", [P, NB])
        pick = sb("pick_gates", [P, P])
        gbias, m0, mprev, mend = sb("gate_bias", [40, 1]), sb("m_start", [HA, SB]), sb("m_prev", [HA, 16]), sb("m_end", [HA, 16])
        wend, wdiag, decb = sb("w_end", [HA, 16]), sb("w_diag", [HA, HA, 16]), sb("decay_all", [P, HA, 16])
        reset = sb("reset", [HA, T])
        ghead = sb("g_head", [P, HA])
        gcur, dcur, ghcur, selcur = sb("gates_now", [P, NB, 3, 2]), sb("decay_now", [P, 16]), sb("g_head_now", [P, 2]), sb("head_now", [HA, 2])
        graw, y, ub, uh = m.sq[0], m.sq[1], m.acc, m.sq[0]
        ig, bsum, mt, stack = num[:, :, :].rearrange("p c e -> p (c e)")[0:HA, 0:T], kT, qT, dec

        w, s = weight_sems(own.sem), norm_sems(own.sem)
        filled, landed = own.sem("fills"), own.sem("a_landed")
        spilled, squares_read = own.sem("h_spilled"), own.sem("h_squares")
        chain, achain = own.sem("dve_step"), own.sem("act_step")
        picked = own.sem("gates_picked")
        y_ready, sp_ready, m_ready, we_in, stack_act = own.sem("softplus_in"), own.sem("softplus_out"), own.sem("m_ready"), own.sem("w_inter_in"), own.sem("stack_act")
        stacked, col_turned, col_ready = own.sem("stack_ready"), own.sem("columns_turned"), own.sem("columns_ready")
        diag_ready, decb_turned = own.sem("w_diag_ready"), own.sem("decay_spread")
        in_turned, in_ready = own.sem("rows_turned"), own.sem("rows_ready")
        qsel_ready, o_exp = own.sem("q_by_sequence_ready"), own.sem("o_exp")
        uh_ready, u_spread, d_ready = own.sem("u_head_ready"), own.sem("u_spread"), own.sem("decay_ready")
        s_ready, wt_ready, kw_ready = own.sem("scores_ready"), own.sem("weighted_ready"), own.sem("kw_ready")
        n1_ready, n2_ready, n2_scaled, num_ready = own.sem("intra_ready"), own.sem("inter_ready"), own.sem("inter_scaled"), own.sem("num_ready")
        dc_ready, c_ready = own.sem("state_add_ready"), own.sem("state_ready")
        dcs_ready, cs_ready = own.sem("state_s_add_ready"), own.sem("state_s_ready")
        h_ready, sq_sum, r_ready, hn_ready = own.sem("head_out"), own.sem("head_squares_ready"), own.sem("head_rms"), own.sem("head_normed")
        out_turned, y_ok = own.sem("head_turned"), own.sem("y_tile")
        state_in, state_out, m_stored = own.sem("state_loaded"), own.sem("state_stored"), own.sem("m_stored")

        win = m.d["w_in_a"][0]
        win_v = win[:, 0:3072].rearrange("(k p) (m j) -> m p k j", p=P, j=P)
        last128 = win[:, 3088 - P:3088].rearrange("(k p) j -> p k j", p=P)
        stages = [(1, [(lambda i: last128, NT), (lambda i: last128, 0)]),
                  (HP, [(lambda i: win_v[i], NT), (lambda i: win_v[i + 4], NT),
                        (lambda i: win_v[i * 2 + 8], NT), (lambda i: win_v[i * 2 + 16], NT),
                        (lambda i: win_v[i * 2 + 9], NT), (lambda i: win_v[i * 2 + 17], NT)])]
        cs_d = m.d["state_c"][0].rearrange("b (p h) k v -> p (h k) b v", h=2)
        ns_d = m.d["state_n"][0].rearrange("b (p h) k -> p (h k) b", h=2)
        cso_d = m.d["c_sample"][0].rearrange("b (p h) k v -> p (h k) b v", h=2)
        nso_d = m.d["n_sample"][0].rearrange("b (p h) k -> p (h k) b", h=2)
        cp_d = m.d["c_prompt"][0, 0].rearrange("(p h) k v -> p (h k) v", h=2)
        np_d = m.d["n_prompt"][0, 0].rearrange("(p h) k -> p (h k)", h=2)
        y_v = m.h[:, :, :].rearrange("p (q h) t -> p q h t", h=2)
        pe_passed = own.sem("pe_passed")
        block = c.enter_context(nc.Block())

        @block.sync
        def _(sp):
            with nc.allow_non_contiguous_dma(reason="gate biases, head gains and stabilisers, 4 KB in all"):
                sp.dma_start(gbias[0:HA, :], m.d["b_i"].rearrange("l h -> h l")).then_inc(landed, 16)
                sp.dma_start(gbias[32:40, :], m.d["b_f"].rearrange("l h -> h l")).then_inc(landed, 16)
                sp.dma_start(m0[:, :], m.d["state_m"][0].rearrange("b h -> h b")).then_inc(landed, 16)
                sp.dma_start(ghead[:, :], m.d["head_norm_a"][0].rearrange("h e -> e h")).then_inc(landed, 16)
            weight_loads(sp, m, w, stages)

        def act_side_loads(act):
            for k in range(KT):
                act.dma_start(m.spill[k], m.h[:, k, :]).then_inc(spilled, 16)

        @block.gpsimd
        def _(pool):
            pool.memset(pick[:, :], 0.0).then_inc(filled, 1)
            pool.memset(stack[:, :], 0.0).then_inc(filled, 1)
            pool.memset(reset[:, :], 1.0).then_inc(filled, 1)
            pool.memset(tokg[:, :, :], 1.0).then_inc(filled, 1)
            pool.memset(vtok[:, :, :, :], 1.0).then_inc(filled, 1)
            pool.memset(qsel[:, :], 0.0).then_inc(filled, 1)
            pool.memset(ss[:, :], 1.0).then_inc(filled, 1)
            pool.wait_ge(filled, 7)
            pool.memset(reset[:, 0:SEQ].rearrange("h (c t) -> h c t", t=P)[:, :, 0:1], 0.0).then_inc(filled, 1)
            pool.memset(reset[:, SEQ:T].rearrange("h (b t) -> h b t", t=ST)[:, :, 0:1], 0.0).then_inc(filled, 1)
            pool.affine_select(out=pick[:, 0:HA], in_=pick[:, 0:HA], compare_op=ALU.not_equal, fill=1.0, base=-112,
                               pattern=[[-1, HA]], channel_multiplier=1).then_inc(filled, 1)
            pool.affine_select(out=pick[:, 32:40], in_=pick[:, 32:40], compare_op=ALU.not_equal, fill=1.0, base=-120,
                               pattern=[[-1, HA]], channel_multiplier=1).then_inc(filled, 1)
            weight_splits(pool, m, w, stages)

        def hr(h2):
            return slice(h2 * DK, (h2 + 1) * DK)

        def toks(cb):
            t0, n = blocks_of(cb)
            return slice(t0, t0 + n)

        @block.tensor
        def _(pe):
            def turn_in(p, g0, tile, src_ready):
                for t in range(NT):
                    pe.wait_ge(w.tile_free[t], src_ready)
                for g, (b0, nb) in enumerate(GROUPS):
                    g += g0
                    pe.wait_ge(in_ready, p * 9 + (g if g == 0 else g - 1))
                    if g < 2:
                        pe.wait_ge(y_ok, p * 6)
                    for j in range(nb):
                        t0, n = blocks_of(b0 + j)
                        last = pe.transpose(m.bank[3 + g % 2][0:n, j * P:(j + 1) * P], tile[:, t0:t0 + n], m.ident[:, :])
                    last.then_inc(in_turned, 1)

            def alone():
                pe.sem_inc(pe_passed, 1)

            def head(p, h2):
                hh = p * 2 + h2
                pe.wait_ge(uh_ready, hh + 1)
                for j, (t0, n) in enumerate(((0, 512), (512, 512), (SEQ, NS))):
                    pe.wait_ge(d_ready, hh * 3 + j)
                    if j < 2:
                        pe.matmul(m.bank[5][:, :], m.ones[0:HA, :], uh[0:HA, t0:t0 + n], start=True, stop=False)
                        last = pe.matmul(m.bank[5][:, :], m.identb[:, :], m.causal[:, :].unsqueeze(1).broadcast_to([P, 4, P]),
                                         start=False, stop=True)
                    else:
                        pe.matmul(m.bank[5][:, 0:NS], m.ones[0:HA, :], uh[0:HA, t0:t0 + n], start=True, stop=False)
                        last = pe.matmul(m.bank[5][:, 0:NS], m.identb[0:NS, :], m.causal_s[:, :], start=False, stop=True)
                    last.then_inc(u_spread, 1)

                def scores(cb):
                    n = blocks_of(cb)[1]
                    pe.wait_ge(wt_ready, hh * NB + cb)
                    if cb == NC:
                        alone()
                    pe.matmul(m.bank[6][0:n, 0:n], kT[hr(h2), toks(cb)], qT[hr(h2), toks(cb)], start=True, stop=True)\
                        .then_inc(s_ready, 1)

                scores(0)
                for cb in range(NB):
                    t0, n = blocks_of(cb)
                    u = hh * NB + cb
                    if cb < NC:
                        scores(cb + 1)
                    pe.wait_ge(y_ok, hh * 3)
                    pe.wait_ge(n2_scaled, u)
                    if cb < NC:
                        pe.wait_ge(c_ready, p * 17 + (h2 * NC + cb + 1))
                        pe.matmul(m.bank[3][0:n, 0:DA], qT[hr(h2), toks(cb)], C[hr(h2), :], start=True, stop=True)\
                            .then_inc(n2_ready, 1)
                    else:
                        pe.wait_ge(state_in, p * 32 + 32)
                        pe.wait_ge(qsel_ready, p + 1)
                        alone()
                        for b in range(SB):
                            last = pe.matmul(m.bank[3][0:n, 0:DA], qsel[hr(h2), b * NS:(b + 1) * NS], Cs[hr(h2), b, :],
                                             start=(b == 0), stop=(b == SB - 1))
                        last.then_inc(n2_ready, 1)
                    pe.wait_ge(num_ready, u)
                    pe.wait_ge(wt_ready, u + 1)
                    if cb == NC:
                        alone()
                    pe.matmul(m.bank[7][0:n, 0:DA], wt[cb % 2][0:n, 0:n], vtok[0:n, cb, h2, :], start=True, stop=True)\
                        .then_inc(n1_ready, 1)
                    if cb < NC:
                        pe.wait_ge(kw_ready, u + 1)
                        pe.matmul(m.bank[4][hr(h2), 0:DA], kw[cb % 2][:, :], vtok[:, cb, h2, :], start=True, stop=True)\
                            .then_inc(dc_ready, 1)
                    else:
                        pe.wait_ge(kw_ready, u + 1)
                        pe.wait_ge(c_ready, p * 17 + (h2 * NC + NC + 1))
                        for g in range(3):
                            pe.wait_ge(cs_ready, hh * 3 + g)
                            for b in range(3 * g, min(3 * g + 3, SB)):
                                last = pe.matmul(m.bank[4][hr(h2), (b % 3) * DA:(b % 3 + 1) * DA], kws[:, b, :],
                                                 vtok[0:NS, NC, h2, :], start=True, stop=True)
                            last.then_inc(dcs_ready, 1)
                pe.wait_ge(hn_ready, hh + 1)
                pe.wait_ge(cs_ready, hh * 3 + 3)
                for g, (b0, nb) in enumerate(OUT_GROUPS):
                    if g == 2:
                        pe.wait_ge(y_ok, hh * 3 + 1)
                    for j in range(nb):
                        n = blocks_of(b0 + j)[1]
                        last = pe.transpose(m.bank[3 + g % 2][:, j * P:j * P + n], num[0:n, b0 + j, 0:DV], m.ident[0:n, 0:n])
                    last.then_inc(out_turned, 1)

            for t in range(NT):
                if t == 0:
                    pe.wait_ge(s.x, KT)
                    pe.wait_ge(w.split, 1)
                dense_tile(pe, m.whi[0], m.wlo[0], KT, 0, m.xhi, m.xlo, t, m.bank[t]).then_inc(w.tile_ready, 1)
            norm_pe(pe, m, s)
            for t in range(NT):
                pe.wait_ge(w.tile_free[t], 1)
            pe.wait_ge(filled, 11)
            pe.wait_ge(s.rs, 1)
            for t in range(NT):
                pe.matmul(m.bank[3 + t][:, 0:TW], pick[:, :], graw[:, t * TW:(t + 1) * TW], start=True, stop=True)\
                    .then_inc(picked, 1)
            pe.wait_ge(stacked, 1)
            for g, (b0, nb) in enumerate(GROUPS):
                for j in range(nb):
                    t0, n = blocks_of(b0 + j)
                    last = pe.transpose(m.bank[3 + g][0:n, j * P:(j + 1) * P], stack[:, t0:t0 + n], m.ident[:, :])
                last.then_inc(col_turned, 1)
            pe.wait_ge(diag_ready, 1)
            pe.matmul(m.bank[6][:, 0:P], m.ones[0:HA, :], wdiag[:, :, :].rearrange("h g e -> h (g e)"), start=True,
                      stop=True).then_inc(decb_turned, 1)
            pe.wait_ge(col_ready, 4)
            with pe.Fori(0, HP) as p:
                dense_panel(pe, m, w, p * 6 + 2, 0, p * 6 + 1)
                dense_panel(pe, m, w, p * 6 + 3, 1, p * 6 + 2)
                dense_panel(pe, m, w, p * 6 + 4, 0, p * 6 + 3)
                dense_panel(pe, m, w, p * 6 + 5, 1, p * 6 + 4)
                turn_in(p, 0, kT, p * 6 + 3)
                turn_in(p, 3, vT, p * 6 + 4)
                dense_panel(pe, m, w, p * 6 + 6, 0, p * 6 + 5)
                dense_panel(pe, m, w, p * 6 + 7, 1, p * 6 + 6)
                turn_in(p, 6, vT, p * 6 + 6)
                pe.wait_ge(in_ready, p * 9 + 9)
                head(p, 0)
                head(p, 1)

        @block.scalar
        def _(act):
            norm_act(act, m, s, m.h, m.g_mix[0])
            act_side_loads(act)
            norm_act_rs(act, m, s)
            step = Pipe(act, achain)
            act.wait_ge(y_ready, 1)
            step(act.activation(bsum[0:HA, :], bsum[0:HA, :], ACT.Exp))
            act.activation(bsum[0:HA, :], bsum[0:HA, :], ACT.Ln, bias=1.0).then_inc(sp_ready, 1)
            act.wait_ge(m_ready, 1)
            act.activation(stack[64:64 + HA, :], mt[0:HA, :], ACT.Exp, scale=-1.0).then_inc(stack_act, 1)
            act.wait_ge(we_in, 1)
            act.activation(stack[32:32 + HA, :], bsum[0:HA, :], ACT.Exp).then_inc(stack_act, 1)
            for g, (b0, nb) in enumerate(GROUPS):
                n = P if g < 2 else NS
                act.wait_ge(col_turned, g + 1)
                act.copy(tokg[0:n, b0:b0 + nb, :],
                         m.bank[3 + g][0:n, :].rearrange("p (j e) -> p j e", e=P)[:, 0:nb, 0:96]).then_inc(col_ready, 1)
            act.wait_ge(decb_turned, 1)
            act.copy(decb[:, :, :].rearrange("p h e -> p (h e)"), m.bank[6][:, 0:P]).then_inc(col_ready, 1)

            def rows(p, g0):
                for g, (b0, nb) in enumerate(GROUPS):
                    n = P if g < 2 else NS
                    g += g0
                    act.wait_ge(in_turned, p * 9 + (g + 1))
                    src = m.bank[3 + g % 2][0:n, :].rearrange("p (j e) -> p j e", e=P)[:, 0:nb, :]
                    dst = ktok[0:n, b0:b0 + nb, :] if g0 == 0 else vtok[0:n, b0:b0 + nb, g0 // 3 - 1, 0:DV]
                    act.copy(dst, src).then_inc(in_ready, 1)

            with act.Fori(0, HP) as p:
                act.wait_ge(state_out, p * 64)
                with nc.allow_non_contiguous_dma(reason="normalisers of the states"):
                    act.dma_start(Cs[:, :, 0:DV], cs_d[p]).then_inc(state_in, 16)
                    act.dma_start(Cs[:, :, DV:DA].rearrange("p b o -> p (b o)"), ns_d[p]).then_inc(state_in, 16)
                for i in range(2):
                    if i == 0:
                        rows(p, 0)
                        rows(p, 3)
                    for t in range(NT):
                        act.wait_ge(w.tile_free[t], p * 6 + (5 if i == 0 else 7))
                    act.activation(gate[i][:, :], gate[i][:, :], ACT.Exp, scale=-1.0).then_inc(o_exp, 1)
                rows(p, 6)
                for h2 in range(2):
                    hh = p * 2 + h2
                    for j in range(3):
                        act.wait_ge(u_spread, hh * 3 + (j + 1))
                        for cb in (range(4 * j, 4 * j + 4) if j < 2 else (NC,)):
                            t0, n = blocks_of(cb)
                            q = (cb % 4) * P
                            last = act.activation(dec[0:n, t0:t0 + n], m.bank[5][0:n, q:q + n], ACT.Exp,
                                                  bias=gcur[0:n, cb, 0, h2:h2 + 1])
                        last.then_inc(d_ready, 1)
                    for cb in range(NB):
                        n = blocks_of(cb)[1]
                        act.wait_ge(n2_ready, hh * NB + (cb + 1))
                        act.wait_ge(num_ready, hh * NB + cb)
                        act.activation(inter[0:n, :], m.bank[3][0:n, 0:DA], ACT.Copy, scale=gcur[0:n, cb, 1, h2:h2 + 1])\
                            .then_inc(n2_scaled, 1)
                    act.wait_ge(h_ready, hh + 1)
                    for cb in range(NB):
                        n = blocks_of(cb)[1]
                        act.activation(sqj[0:n, :], num[0:n, cb, 0:DV], ACT.Square, accum_out=ss[0:n, cb:cb + 1])\
                            .then_inc(sq_sum, 1)
                        act.wait_ge(sq_sum, hh * NB + (cb + 1))
                    act.activation(ss[:, :], ss[:, :], ACT.Ln, bias=m.eps[:, 0:1], scale=1.0 / DV).then_inc(r_ready, 1)
                    act.wait_ge(r_ready, hh * 2 + 1)
                    act.activation(ss[:, :], ss[:, :], ACT.Exp, scale=-0.5).then_inc(r_ready, 1)
                act.wait_ge(cs_ready, p * 6 + 6)
                act.wait_ge(c_ready, p * 17 + 17)
                with nc.allow_non_contiguous_dma(reason="normalisers of the states"):
                    act.dma_start(cp_d[p], C[:, 0:DV]).then_inc(state_out, 16)
                    act.dma_start(np_d[p].rearrange("(q o) -> q o", o=1), C[:, DV:DA]).then_inc(state_out, 16)
                    act.dma_start(cso_d[p], Cs[:, :, 0:DV]).then_inc(state_out, 16)
                    act.dma_start(nso_d[p], Cs[:, :, DV:DA].rearrange("p b o -> p (b o)")).then_inc(state_out, 16)
            act.wait_ge(state_out, 64 * HP)
            act.dma_start(m.d["m_prompt"][0].rearrange("o h -> h o"), mend[:, NC - 1:NC]).then_inc(m_stored, 16)
            with nc.allow_non_contiguous_dma(reason="256 bytes"):
                act.dma_start(m.d["m_sample"][0].rearrange("b h -> h b"), mend[:, NC:16]).then_inc(m_stored, 16)
            act.wait_ge(m_stored, 32)
            act.wait_ge(spilled, 16 * KT)

        @block.vector
        def _(dve):
            norm_dve(dve, m, s, m.h, m.g_mix[0])
            step = Pipe(dve, chain)
            dve.wait_ge(s.rs, 1)
            for t in range(NT):
                ts = slice(t * TW, (t + 1) * TW)
                dve.wait_ge(w.tile_ready, t + 1)
                ins = dve.tensor_tensor(graw[:, ts], m.bank[t][:, 0:TW], m.rs[:, ts], ALU.mult)
                ins.then_inc(w.tile_free[t], 1)
            dve.wait_ge(landed, 64)
            dve.wait_ge(filled, 11)
            dve.wait_ge(picked, NT)
            for t in range(NT):
                ts = slice(t * TW, (t + 1) * TW)
                dve.tensor_scalar(ig[:, ts], m.bank[3 + t][0:HA, 0:TW], gbias[0:HA, 0:1], None, ALU.add)
                step(dve.tensor_scalar(y[0:HA, ts], m.bank[3 + t][32:32 + HA, 0:TW], gbias[32:32 + HA, 0:1], -1.0,
                                       ALU.add, ALU.mult))
            dve.tensor_scalar(bsum[0:HA, :], y[0:HA, :], CLAMP, None, ALU.min).then_inc(y_ready, 1)
            dve.wait_ge(sp_ready, 1)
            step(dve.tensor_tensor(y[0:HA, :], y[0:HA, :], bsum[0:HA, :], ALU.max))
            step(dve.tensor_scalar(y[0:HA, :], y[0:HA, :], -1.0, None, ALU.mult))
            dve.tensor_tensor_scan(bsum[0:HA, :], reset[:, :], y[0:HA, :], 0.0, ALU.mult, ALU.add)
            step(dve.tensor_tensor_scan(mt[0:HA, 0:SEQ], y[0:HA, 0:SEQ], ig[:, 0:SEQ], 0.0, ALU.add, ALU.max))
            for b in range(SB):
                bt = slice(SEQ + b * ST, SEQ + (b + 1) * ST)
                last = dve.tensor_tensor_scan(mt[0:HA, bt], y[0:HA, bt], ig[:, bt], m0[:, b:b + 1], ALU.add, ALU.max)
            last.then_inc(m_ready, 1)
            dve.wait_ge(m_ready, 1)

            def ends(ap):
                return (ap[:, 0:SEQ].rearrange("h (c t) -> h c t", t=P)[:, :, P - 1],
                        ap[:, SEQ:T].rearrange("h (b t) -> h b t", t=ST)[:, :, ST - 1])

            a, b_ = ends(mt[0:HA, :])
            dve.tensor_copy(mend[:, 0:NC], a)
            step(dve.tensor_copy(mend[:, NC:16], b_))
            dve.memset(mprev[:, 0:1], 0.0)
            dve.tensor_copy(mprev[:, 1:NC], mend[:, 0:NC - 1])
            dve.tensor_copy(mprev[:, NC:16], m0[:, :])
            dve.tensor_tensor(stack[0:HA, :], ig[:, :], bsum[0:HA, :], ALU.subtract)
            step(dve.tensor_tensor(ub[0:HA, :], bsum[0:HA, :], mt[0:HA, :], ALU.subtract))
            dve.tensor_tensor(bsum[0:HA, 0:SEQ].rearrange("h (c t) -> h c t", t=P),
                              ub[0:HA, 0:SEQ].rearrange("h (c t) -> h c t", t=P),
                              mprev[:, 0:NC].unsqueeze(2).broadcast_to([HA, NC, P]), ALU.add)
            dve.tensor_tensor(bsum[0:HA, SEQ:T].rearrange("h (c t) -> h c t", t=ST),
                              ub[0:HA, SEQ:T].rearrange("h (c t) -> h c t", t=ST),
                              mprev[:, NC:16].unsqueeze(2).broadcast_to([HA, SB, ST]), ALU.add).then_inc(we_in, 1)
            dve.wait_ge(stack_act, 2)
            a, b_ = ends(stack[32:32 + HA, :])
            dve.tensor_copy(wend[:, 0:NC], a).then_inc(stacked, 1)
            step(dve.tensor_copy(wend[:, NC:16], b_))
            dve.tensor_tensor(wdiag[:, :, :], wend[:, :].unsqueeze(1).broadcast_to([HA, HA, 16]),
                              m.ident[0:HA, 0:HA].unsqueeze(2).broadcast_to([HA, HA, 16]), ALU.mult).then_inc(diag_ready, 1)
            step(dve.memset(num[:, :, :], 0.0))
            dve.wait_ge(col_ready, 4)

            def read_out(p, j, dst, scale=None):
                for t in range(NT):
                    ts = slice(t * TW, (t + 1) * TW)
                    dve.wait_ge(w.tile_ready, p * 18 + (3 * j + t + 4))
                    if scale is None:
                        ins = dve.tensor_tensor(dst[:, ts], m.bank[t][:, 0:TW], m.rs[:, ts], ALU.mult)
                    else:
                        ins = dve.scalar_tensor_tensor(out=dst[:, ts], in0=m.bank[t][:, 0:TW], scalar=scale,
                                                       in1=m.rs[:, ts], op0=ALU.mult, op1=ALU.mult)
                    ins.then_inc(w.tile_free[t], 1)

            def post(p, h2):
                hh = p * 2 + h2
                step(dve.scalar_tensor_tensor(out=den[:, :], in0=num[:, :, DV], scalar=-1.0, in1=num[:, :, DV],
                                              op0=ALU.mult, op1=ALU.max))
                step(dve.tensor_tensor(den[:, :], den[:, :], gcur[:, :, 2, h2], ALU.max))
                step(dve.reciprocal(den[:, :], den[:, :]))
                hv = num[:, :, 0:DV]
                dve.tensor_tensor(hv, hv, den[:, :].unsqueeze(2).broadcast_to([P, NB, DV]), ALU.mult).then_inc(h_ready, 1)
                dve.wait_ge(r_ready, hh * 2 + 2)
                dve.tensor_tensor(hv, hv, ss[:, :].unsqueeze(2).broadcast_to([P, NB, DV]), ALU.mult).then_inc(hn_ready, 1)
                for g, (b0, nb) in enumerate(OUT_GROUPS):
                    dve.wait_ge(out_turned, hh * 3 + (g + 1))
                    t0, n = (b0 * P, nb * P) if b0 < NC else (SEQ, NS)
                    dve.scalar_tensor_tensor(out=y_v[:, bass.ds(p, 1), h2, t0:t0 + n].rearrange("p q t -> p (q t)"),
                                             in0=m.bank[3 + g % 2][:, 0:n], scalar=ghcur[:, h2:h2 + 1],
                                             in1=gate[h2][:, t0:t0 + n], op0=ALU.mult, op1=ALU.mult).then_inc(y_ok, 1)

            dve.wait_ge(spilled, 16 * KT)
            with dve.Fori(0, HP) as p:
                step.enter(p, 11)
                dve.wait_ge(state_out, p * 64)
                dve.wait_ge(y_ok, p * 6)
                dve.memset(C[:, :], 0.0).then_inc(c_ready, 1)
                dve.tensor_copy(gcur[:, :, :, :], tokg[:, :, :].rearrange("p c (g e) -> p c g e", g=3)[:, :, :, bass.ds(p * 2, 2)])
                dve.tensor_copy(dcur[0:DK, :], decb[0:DK, bass.ds(p * 2, 1), :].rearrange("p o e -> p (o e)"))
                dve.tensor_copy(dcur[DK:P, :], decb[DK:P, bass.ds(p * 2 + 1, 1), :].rearrange("p o e -> p (o e)"))
                dve.tensor_copy(ghcur[:, :], ghead[:, bass.ds(p * 2, 2)])
                step(dve.tensor_copy(selcur[:, :], m.ident[0:HA, bass.ds(p * 2, 2)]))
                read_out(p, 0, qT)
                dve.wait_ge(w.tile_free[NT - 1], p * 6 + 2)
                dve.tensor_copy(qsel[:, :].rearrange("p (b t) -> p b t", t=NS + ST)[:, :, 0:ST],
                                qT[:, SEQ:T].rearrange("p (b t) -> p b t", t=ST)).then_inc(qsel_ready, 1)
                read_out(p, 1, kT, DK ** -0.5)
                read_out(p, 2, vT)
                read_out(p, 3, gate[0])
                dve.wait_ge(in_turned, p * 9 + 6)
                read_out(p, 4, vT)
                read_out(p, 5, gate[1])
                for i in range(2):
                    dve.wait_ge(o_exp, p * 2 + (i + 1))
                    step(dve.tensor_scalar(gate[i][:, :], gate[i][:, :], 1.0, None, ALU.add))
                    step(dve.reciprocal(gate[i][:, :], gate[i][:, :]))
                dve.wait_ge(in_ready, p * 9 + 9)
                for h2 in range(2):
                    hh = p * 2 + h2
                    dve.wait_ge(u_spread, hh * 3)
                    dve.tensor_scalar(uh[0:HA, :], ub[0:HA, :], selcur[:, h2:h2 + 1], None, ALU.mult).then_inc(uh_ready, 1)
                    for cb in range(NB + 1):
                        u = hh * NB + cb
                        if cb < NB:
                            t0, n = blocks_of(cb)
                            dve.wait_ge(d_ready, hh * 3 + (cb // 4 + 1))
                            dve.wait_ge(s_ready, u + 1)
                            dve.wait_ge(n1_ready, u if cb == 0 else hh * NB + (cb - 1))
                            dve.tensor_tensor(wt[cb % 2][0:n, 0:n], m.bank[6][0:n, 0:n], dec[0:n, t0:t0 + n], ALU.mult)\
                                .then_inc(wt_ready, 1)
                            if cb < NC:
                                if cb == 0:
                                    dve.wait_ge(dc_ready, hh * NC)
                                dve.tensor_scalar(kw[cb % 2][:, :], ktok[:, cb, hr(h2)], dec[:, t0 + P - 1:t0 + P], None,
                                                  ALU.mult).then_inc(kw_ready, 1)
                            else:
                                dve.wait_ge(dcs_ready, hh * 3)
                                lastcol = dec[0:NS, SEQ:T].rearrange("s (b t) -> s b t", t=ST)[:, :, ST - 1:ST]
                                dve.tensor_tensor(kws[:, :, :],
                                                  ktok[0:NS, NC, hr(h2)].unsqueeze(1).broadcast_to([NS, SB, DK]),
                                                  lastcol.broadcast_to([NS, SB, DK]), ALU.mult).then_inc(kw_ready, 1)
                        if cb >= 1:
                            pb = cb - 1
                            n = blocks_of(pb)[1]
                            if pb < NC:
                                dve.wait_ge(dc_ready, hh * NC + (pb + 1))
                                dve.scalar_tensor_tensor(out=C[hr(h2), :], in0=C[hr(h2), :], scalar=dcur[hr(h2), pb:pb + 1],
                                                         in1=m.bank[4][hr(h2), 0:DA], op0=ALU.mult, op1=ALU.add)\
                                    .then_inc(c_ready, 1)
                            dve.wait_ge(n1_ready, hh * NB + (pb + 1))
                            dve.wait_ge(n2_scaled, hh * NB + (pb + 1))
                            dve.tensor_tensor(num[0:n, pb, :], m.bank[7][0:n, 0:DA], inter[0:n, :], ALU.add)\
                                .then_inc(num_ready, 1)
                    for g in range(3):
                        dve.wait_ge(dcs_ready, hh * 3 + (g + 1))
                        for b in range(3 * g, min(3 * g + 3, SB)):
                            j = b % 3
                            last = dve.scalar_tensor_tensor(out=Cs[hr(h2), b, :], in0=Cs[hr(h2), b, :],
                                                            scalar=dcur[hr(h2), NC + b:NC + b + 1],
                                                            in1=m.bank[4][hr(h2), j * DA:(j + 1) * DA],
                                                            op0=ALU.mult, op1=ALU.add)
                        last.then_inc(cs_ready, 1)
                    dve.wait_ge(num_ready, hh * NB + NB)
                    post(p, h2)
            step.leave(HP)


def mixer_b(nc, m, own):
    U = 24
    G0, GROUPS = 4, [(0, 4), (4, 4), (8, 1)]
    SLOTS = 4
    units = []
    for tt in range(2):
        for h2 in range(2):
            blocks = list(range(4 * tt + 3, -1, -1))
            for kb in blocks:
                units.append((h2, tt, kb, max(0, kb - 4 * tt) * P, kb == blocks[0], kb == 0))
    assert len(units) == U
    run_end = {i: r for r, i in enumerate(i for i, u in enumerate(units) if u[5])}
    TURN, Z_IN, SP_OUT, CUM, PV0 = 1, 10, 11, 12, 13
    with ExitStack() as c:
        sb = own.tensor

        qT, kT, vT = sb("q_t", [P, T]), sb("k_t", [P, T]), sb("v_t", [P, T])
        krow, vrow = sb("k_rows", [P, NB, P]), sb("v_rows", [P, NB, P])
        zc = [sb(f"softplus{i}", [P, 512]) for i in range(2)]
        sp = [sb(f"sp{i}", [P, 512]) for i in range(2)]
        later = [sb(f"sp_later{i}", [P, 512]) for i in range(2)]
        a = [sb(f"weights{i}", [P, 512]) for i in range(2)]
        pages = [sb(f"pages{i}", [P, NPG, P]) for i in range(SLOTS)]
        kpT = [sb(f"page_keys_t{i}", [P, NPG * PAGE]) for i in range(2)]
        zcs, sps, laters, as_ = m.sq[0][:, 0:512], m.sq[1][:, 0:512], m.acc[:, 0:512], m.sq[0][:, 512:1024]
        zcn, spn, an = sb("softplus_new", [NS, 2 * NS]), sb("sp_new", [NS, 2 * NS]), sb("weights_new", [NS, 2 * NS])
        qd = sb("q_sample", [P, SB, 2, ST])
        bias, bcur = sb("bias", [P, HB]), sb("bias_now", [P, 2])
        ptab = sb("page_table", [1, SB * NPG], I32)

        w, s = weight_sems(own.sem), norm_sems(own.sem)
        landed, spilled, filled, chain = own.sem("b_landed"), own.sem("h_spilled"), own.sem("fills"), own.sem("dve_step")
        ptab_in = own.sem("page_table_in")
        in_turned, in_ready = own.sem("rows_turned"), own.sem("rows_ready")
        stored = own.sem("rows_stored")
        z_ready, zc_ready, e_ready, ln_ready = own.sem("z_ready"), own.sem("z_clamped"), own.sem("exp_ready"), own.sem("ln_ready")
        sp_ready, later_ready = own.sem("sp_ready"), own.sem("sp_later_ready")
        cum_ready, a_ready, pv_ready, y_ok = own.sem("sums_ready"), own.sem("weights_ready"), own.sem("pv_ready"), own.sem("y_tile")
        page_in = [own.sem(f"pages_in{i}") for i in range(SLOTS)]
        k_turned, kt_act, kt_dve, zs_done = own.sem("keys_turned"), own.sem("keys_t_low"), own.sem("keys_t_high"), own.sem("zs_by_seq")
        pvs_done = own.sem("pvs_by_seq")
        qd_ready, zs_ready, zcs_ready, es_ready = own.sem("q_sample_ready"), own.sem("zs_ready"), own.sem("zs_clamped"), own.sem("es_ready")
        lns_ready, sps_ready, cums_ready, as_ready = own.sem("lns_ready"), own.sem("sps_ready"), own.sem("sums_s_ready"), own.sem("weights_s_ready")
        ys_ok = own.sem("ys_tile")
        pe_passed, sp_passed = own.sem("pe_passed"), own.sem("sp_passed")

        wq_v = m.d["w_q_b"][0].rearrange("(k p) (m j) -> m p k j", p=P, j=P)
        wkv_v = m.d["w_kv"].rearrange("(k p) (m j) -> m p k j", p=P, j=P)
        panels = []
        for pp in range(2):
            panels += [(lambda i, pp=pp: wq_v[i * 2 + pp], NT, m.g_mix[1]),
                       (lambda i, pp=pp: wkv_v[i * 2 + pp], NT, m.g_kv),
                       (lambda i, pp=pp: wkv_v[i * 2 + (pp + 8)], NT, m.g_kv)]
        kp_d, vp_d = (x[0].rearrange("(c p) (q h) e -> q p c (h e)", p=P, h=2) for x in (m.d["k_prompt"], m.d["v_prompt"]))
        ks_d, vs_d = (x.rearrange("b t (q h) e -> q (b t) (h e)", h=2) for x in (m.d["k_sample"], m.d["v_sample"]))
        ck_d, cv_d = (x.rearrange("n s (q h) e -> q n s (h e)", h=2) for x in (m.d["cache_k"], m.d["cache_v"]))
        y_v = m.h[:, :, :]
        block = c.enter_context(nc.Block())

        def hr(h2):
            return slice(h2 * DH, (h2 + 1) * DH)

        def by_page(ap):
            return ap.rearrange("p (x g t) -> p x g t", g=NPG, t=ST)

        @block.sync
        def _(eng):
            eng.dma_start(ptab[:, :], m.d["page_table"].rearrange("b (o g) -> o (b g)", o=1)).then_inc(ptab_in, 16)
            eng.dma_start(bias[:, :], m.d["sb_bias"][0:1, :].broadcast_to([P, HB]))\
                .then_inc(landed, 16)

            def weights(i, j):
                n = i * 6 + j
                if not isinstance(n, int) or n >= 2:
                    eng.wait_ge(w.split, n - 1)
                ap = panels[j % 6][0](i if j < 6 else i + 1)
                eng.dma_start(m.wraw[j % 2][:, :].rearrange("p (k j) -> p k j", j=P), ap).then_inc(w.loaded[j % 2], 16)

            for j in range(3):
                weights(0, j)
            for k in range(KT):
                eng.dma_start(m.spill[k], m.h[:, k, :]).then_inc(spilled, 16)
            eng.wait_ge(ptab_in, 16)

            def cached(i, pp, src, first):
                pair = i * 2 + pp
                with eng.Fori(0, SB // SLOTS) as r:
                    for x in range(SLOTS):
                        if first == 0:
                            eng.wait_ge(k_turned, pair * 16 + r * (2 * x + 2))
                            eng.sem_inc(sp_passed, 1)
                            eng.wait_ge(pvs_done, pair * 8 + (x + 5))
                        else:
                            eng.wait_ge(k_turned, pair * 16 + (2 * (SLOTS + x) + 2))
                            eng.sem_inc(sp_passed, 1)
                            eng.wait_ge(pvs_done, pair * 8 + r * (x + 1) + 8)
                        eng.sem_inc(sp_passed, 1)
                        for g in range(NPG):
                            page = eng.value_load(ptab[0:1, bass.ds(r * (SLOTS * NPG) + (x * NPG + g), 1)],
                                                  min_val=0, max_val=m.d["cache_k"].shape[0] - 1)
                            eng.dma_start(pages[x][:, g, :], src[pair, page]).then_inc(page_in[x], 16)

            def pair_loads(i, pp, more):
                pair = i * 2 + pp
                cached(i, pp, ck_d, 0)
                if more:
                    for j in range(3):
                        weights(i, 3 * pp + 3 + j)
                eng.wait_ge(in_ready, pair * 6 + 6)
                eng.dma_start(kp_d[pair], krow[:, 0:NC, :]).then_inc(stored, 16)
                eng.dma_start(vp_d[pair], vrow[:, 0:NC, :]).then_inc(stored, 16)
                eng.dma_start(ks_d[pair], krow[0:NS, NC, :]).then_inc(stored, 16)
                eng.dma_start(vs_d[pair], vrow[0:NS, NC, :]).then_inc(stored, 16)
                cached(i, pp, cv_d, 8)

            with eng.Fori(0, HB // 4 - 1) as i:
                for pp in range(2):
                    pair_loads(i, pp, True)
            pair_loads(HB // 4 - 1, 0, True)
            pair_loads(HB // 4 - 1, 1, False)
            eng.wait_ge(stored, 64 * (HB // 2))
            eng.wait_ge(spilled, 16 * KT)

        @block.gpsimd
        def _(pool):
            pool.memset(qd[:, :, :, :], 0.0).then_inc(filled, 1)
            weight_splits(pool, m, w, [(HB // 4, panels)])

        @block.tensor
        def _(pe):
            def turn_in(pair, g0, tile, used):
                for t in range(NT):
                    pe.wait_ge(w.tile_free[t], used)
                for g, (b0, nb) in enumerate(GROUPS):
                    g += g0
                    pe.wait_ge(in_ready, pair * 6 + max(g - 1, 0))
                    for j in range(nb):
                        t0, n = blocks_of(b0 + j)
                        last = pe.transpose(m.bank[3 + g % 2][0:n, j * P:(j + 1) * P], tile[:, t0:t0 + n], m.ident[:, :])
                    last.then_inc(in_turned, 1)

            def z(pair, i):
                h2, tt, kb, off, _, _ = units[i]
                if i >= 3:
                    pe.wait_ge(a_ready, pair * U + (i - 2))
                q0 = tt * 512 + off
                pe.matmul(m.bank[3 + i % 3][:, 0:512 - off], kT[hr(h2), kb * P:(kb + 1) * P],
                          qT[hr(h2), q0:tt * 512 + 512], start=True, stop=True).then_inc(z_ready, 1)

            def sums(pair, i):
                h2, tt, kb, off, first, _ = units[i]
                n, bank = 512 - off, m.bank[3 + i % 3]
                pe.wait_ge(sp_ready, pair * U + (i + 1))
                last = pe.matmul(bank[:, 0:n], m.negtri[:, :], sp[i % 2][:, 0:n], start=False, stop=True,
                                 skip_group_check=True)
                diagonal = kb >= 4 * tt
                if not first:
                    pe.wait_ge(later_ready, pair * U + i)
                    skip = P if diagonal else 0
                    last = pe.matmul(bank[:, skip:n], m.negones[:, :], later[(i - 1) % 2][:, off + skip:512], start=False,
                                     stop=True, skip_group_check=True)
                if diagonal:
                    last = pe.matmul(bank[:, 0:P], m.identb[:, :], m.strict[:, :], start=False, stop=True,
                                     skip_group_check=True)
                last.then_inc(cum_ready, 1)

            def pv(pair, i):
                h2, tt, kb, off, first, last = units[i]
                pe.wait_ge(a_ready, pair * U + (i + 1))
                if first:
                    pe.wait_ge(y_ok, pair * 4 + (0 if tt == 0 else 1 + h2))
                pe.matmul(m.bank[6][hr(h2), off:512], vrow[:, kb, hr(h2)], a[i % 2][:, 0:512 - off], start=first, stop=last,
                          skip_group_check=True).then_inc(pv_ready, 1)

            def turn_pages(pair, b):
                pe.wait_ge(page_in[b % SLOTS], pair * 512 + (b // SLOTS + 1) * 128)
                for half in range(2):
                    pe.wait_ge(kt_dve if half else kt_act, pair * SB + b)
                    for g in range(4):
                        last = pe.transpose(m.bank[half][:, g * P:(g + 1) * P], pages[b % SLOTS][:, 4 * half + g, :],
                                            m.ident[:, :])
                    last.then_inc(k_turned, 1)

            def z_pages(pair, b):
                pe.wait_ge(kt_act, pair * SB + (b + 1))
                pe.wait_ge(kt_dve, pair * SB + (b + 1))
                if b == 0:
                    pe.wait_ge(qd_ready, pair * 2 + 2)
                    pe.wait_ge(as_ready, pair * 4)
                for g in range(NPG):
                    out = m.bank[7][:, :].rearrange("p (h x) -> p h x", h=2)[:, :, b * 32 + g * ST:b * 32 + g * ST + ST]
                    last = pe.matmul(out, kpT[b % 2][:, g * PAGE:(g + 1) * PAGE], qd[:, b, :, :], start=(b == 0 and g == 0),
                                     stop=True, skip_group_check=True)
                last.then_inc(zs_done, 1)

            def z_new(pair):
                pe.matmul(m.bank[2][0:NS, 0:2 * NS].rearrange("p (h b t) -> p h b t", h=2, t=ST), kT[:, SEQ:T], qd[:, :, :, :].rearrange("p b h t -> p h b t"),
                          start=True, stop=True).then_inc(zs_ready, 1)

            def sums_s(pair):
                pe.wait_ge(sps_ready, pair * 2 + 2)
                pe.matmul(m.bank[7][:, :], m.negtri[:, :], sps, start=False, stop=True, skip_group_check=True)
                pe.matmul(by_page(m.bank[7][:, :])[:, :, 0:NPG - 1, :], m.negones[:, :],
                          by_page(laters)[:, :, 0:NPG - 1, :], start=False, stop=True, skip_group_check=True)
                pe.matmul(by_page(m.bank[7][:, :]), m.negones[0:NS, :],
                          spn[:, :].rearrange("s (x t) -> s x t", t=ST).unsqueeze(2).broadcast_to([NS, 2 * SB, NPG, ST]),
                          start=False, stop=True, skip_group_check=True).then_inc(cums_ready, 1)
                pe.matmul(m.bank[2][0:NS, 0:2 * NS], m.negtri[0:NS, 0:NS], spn[:, :], start=False, stop=True, skip_group_check=True)
                pe.matmul(m.bank[2][0:NS, 0:2 * NS], m.identb[0:NS, 0:NS], m.new_mask[:, :], start=False, stop=True,
                          skip_group_check=True).then_inc(cums_ready, 1)

            def pv_pages(pair, b):
                if b == 0:
                    pe.wait_ge(as_ready, pair * 4 + 4)
                    pe.wait_ge(kt_act, pair * SB + SB)
                pe.wait_ge(page_in[b % SLOTS], pair * 512 + (2 + b // SLOTS + 1) * 128)
                heads = as_[:, :].rearrange("p (h x) -> p h x", h=2)
                for g in range(NPG):
                    c0 = b * 32 + g * ST
                    pe.matmul(m.bank[0][:, b * 8:b * 8 + 8].rearrange("p (h t) -> p h t", h=2), pages[b % SLOTS][:, g, :], heads[:, :, c0:c0 + ST],
                              start=(b == 0 and g == 0), stop=False, skip_group_check=True)
                pe.matmul(m.bank[0][:, b * 8:b * 8 + 8].rearrange("p (h t) -> p h t", h=2), vrow[0:NS, NC, :],
                          an[:, :].rearrange("s (h b t) -> s h b t", h=2, b=SB)[:, :, b, :], start=False, stop=True,
                          skip_group_check=True).then_inc(pvs_done, 1)

            pe.sem_inc(pvs_done, SB)
            norm_pe(pe, m, s)
            with pe.Fori(0, HB // 4) as i2:
                for pp in range(2):
                    pair = i2 * 2 + pp
                    if pp == 0:
                        pe.wait_ge(ys_ok, i2 * 4)
                    else:
                        pe.wait_ge(ys_ok, i2 * 4 + 2)
                    for j in range(3):
                        if j == 0:
                            pe.wait_ge(s.x, KT)
                        dense_panel(pe, m, w, i2 * 6 + (3 * pp + j), (3 * pp + j) % 2, i2 * 6 + (3 * pp + j))
                    turn_in(pair, 0, kT, i2 * 6 + (3 * pp + 2))
                    turn_in(pair, 3, vT, i2 * 6 + (3 * pp + 3))
                    pe.wait_ge(in_ready, pair * 6 + 6)
                    z(pair, 0)
                    z(pair, 1)
                    for i in range(U):
                        sums(pair, i)
                        if i + 2 < U:
                            z(pair, i + 2)
                        if i >= 1:
                            pv(pair, i - 1)
                        if TURN + 1 <= i < TURN + 1 + SB:
                            z_pages(pair, i - TURN - 1)
                        if TURN <= i < TURN + SB:
                            turn_pages(pair, i - TURN)
                        if i == TURN + SB:
                            z_new(pair)
                        if i == CUM:
                            sums_s(pair)
                        if PV0 <= i < PV0 + SB:
                            pv_pages(pair, i - PV0)
                    pv(pair, U - 1)

        @block.scalar
        def _(act):
            norm_act(act, m, s, m.h, None)
            norm_act_rs(act, m, s)

            def rows(pair, g0, dst):
                for g, (b0, nb) in enumerate(GROUPS):
                    n = P if g < 2 else NS
                    act.wait_ge(in_turned, pair * 6 + (g + g0 + 1))
                    src = m.bank[3 + (g + g0) % 2][0:n, :].rearrange("p (j e) -> p j e", e=P)[:, 0:nb, :]
                    act.copy(dst[0:n, b0:b0 + nb, :], src).then_inc(in_ready, 1)

            def softplus(pair, i):
                n = 512 - units[i][3]
                act.wait_ge(zc_ready, pair * U + (i + 1))
                act.activation(zc[i % 2][:, 0:n], zc[i % 2][:, 0:n], ACT.Exp).then_inc(e_ready, 1)
                act.wait_ge(e_ready, pair * U + (i + 1))
                act.activation(zc[i % 2][:, 0:n], zc[i % 2][:, 0:n], ACT.Ln, bias=1.0).then_inc(ln_ready, 1)

            def weights(pair, i):
                h2, n = units[i][0], 512 - units[i][3]
                act.wait_ge(cum_ready, pair * U + (i + 1))
                if i >= 2:
                    act.wait_ge(pv_ready, pair * U + (i - 1))
                act.activation(a[i % 2][:, 0:n], m.bank[3 + i % 3][:, 0:n], ACT.Exp, bias=bcur[:, h2:h2 + 1])\
                    .then_inc(a_ready, 1)

            with act.Fori(0, HB // 4) as i2:
                for pp in range(2):
                    pair = i2 * 2 + pp
                    act.wait_ge(stored, pair * 64)
                    rows(pair, 0, krow)
                    rows(pair, 3, vrow)
                    softplus(pair, 0)
                    for i in range(U):
                        if i + 1 < U:
                            softplus(pair, i + 1)
                        weights(pair, i)
                        if TURN <= i < TURN + SB:
                            b = i - TURN
                            act.wait_ge(k_turned, pair * 16 + (2 * b + 1))
                            if b >= 2:
                                act.wait_ge(zs_done, pair * SB + (b - 1))
                            act.copy(kpT[b % 2][:, 0:512], m.bank[0][:, :]).then_inc(kt_act, 1)
                        if i == Z_IN:
                            for j, tile in enumerate((zcs, zcn[:, :])):
                                act.wait_ge(zcs_ready, pair * 4 + (2 * j + 2))
                                act.activation(tile, tile, ACT.Exp).then_inc(es_ready, 1)
                                act.wait_ge(es_ready, pair * 2 + (j + 1))
                                act.activation(tile, tile, ACT.Ln, bias=1.0).then_inc(lns_ready, 1)
                        if i == CUM:
                            for h2 in range(2):
                                if h2 == 0:
                                    act.wait_ge(cums_ready, pair * 2 + 2)
                                half, nh = slice(256 * h2, 256 * h2 + 256), slice(NS * h2, NS * h2 + NS)
                                act.activation(as_[:, half], m.bank[7][:, half], ACT.Exp, bias=bcur[:, h2:h2 + 1])\
                                    .then_inc(as_ready, 1)
                                act.activation(an[:, nh], m.bank[2][0:NS, nh], ACT.Exp, bias=bcur[0:NS, h2:h2 + 1])\
                                    .then_inc(as_ready, 1)

        @block.vector
        def _(dve):
            norm_dve(dve, m, s, m.h, None)
            step = Pipe(dve, chain)
            dve.wait_ge(landed, 16)
            dve.wait_ge(filled, 1)
            dve.wait_ge(spilled, 16 * KT)
            dve.wait_ge(s.rs, 1)

            def read_out(i2, j, dst, scale=None):
                for t in range(NT):
                    ts = slice(t * TW, (t + 1) * TW)
                    dve.wait_ge(w.tile_ready, i2 * 18 + (3 * j + t + 1))
                    if scale is None:
                        ins = dve.tensor_tensor(dst[:, ts], m.bank[t][:, 0:TW], m.rs[:, ts], ALU.mult)
                    else:
                        ins = dve.scalar_tensor_tensor(out=dst[:, ts], in0=m.bank[t][:, 0:TW], scalar=scale,
                                                       in1=m.rs[:, ts], op0=ALU.mult, op1=ALU.mult)
                    ins.then_inc(w.tile_free[t], 1)

            def clamp(pair, i):
                h2, n = units[i][0], 512 - units[i][3]
                dve.wait_ge(z_ready, pair * U + (i + 1))
                if i >= 2:
                    dve.wait_ge(sp_ready, pair * U + (i - 1))
                dve.tensor_scalar(zc[i % 2][:, 0:n], m.bank[3 + i % 3][:, 0:n], bcur[:, h2:h2 + 1], CLAMP, ALU.add, ALU.min)\
                    .then_inc(zc_ready, 1)

            def softplus(pair, i):
                h2, tt, kb, off, first, last = units[i]
                n = 512 - off
                dve.wait_ge(ln_ready, pair * U + (i + 1))
                if i >= 2:
                    dve.wait_ge(cum_ready, pair * U + (i - 1))
                args = dict(out=sp[i % 2][:, 0:n], in0=m.bank[3 + i % 3][:, 0:n], scalar=bcur[:, h2:h2 + 1],
                            in1=zc[i % 2][:, 0:n], op0=ALU.add, op1=ALU.max)
                if kb >= 4 * tt:
                    step(dve.scalar_tensor_tensor(**args))
                    dve.tensor_tensor(sp[i % 2][:, 0:P], sp[i % 2][:, 0:P], m.strict01[:, :], ALU.mult).then_inc(sp_ready, 1)
                else:
                    dve.scalar_tensor_tensor(**args).then_inc(sp_ready, 1)
                dve.wait_ge(sp_ready, pair * U + (i + 1))
                if i:
                    dve.wait_ge(cum_ready, pair * U + i)
                    dve.wait_ge(later_ready, pair * U + i)
                new, old = later[i % 2], later[(i - 1) % 2]
                if first:
                    dve.tensor_copy(new[:, off:512], sp[i % 2][:, 0:n]).then_inc(later_ready, 1)
                    return
                skip = P if kb >= 4 * tt else 0
                if skip:
                    dve.tensor_copy(new[:, off:off + P], sp[i % 2][:, 0:P])
                dve.tensor_tensor(new[:, off + skip:512], old[:, off + skip:512], sp[i % 2][:, skip:n], ALU.add)\
                    .then_inc(later_ready, 1)

            def run_out(pair, r):
                h2, tt = r % 2, r // 2
                last = [i for i, q in run_end.items() if q == r][0]
                dve.wait_ge(pv_ready, pair * U + (last + 1))
                dve.tensor_copy(y_v[hr(h2), bass.ds(pair, 1), tt * 512:tt * 512 + 512].rearrange("p o t -> p (o t)"),
                                m.bank[6][hr(h2), :]).then_inc(y_ok, 1)

            with dve.Fori(0, HB // 4) as i2:
                step.enter(i2, 2 * (1 + 16 + 2 + 1 + NPG - 3))
                for pp in range(2):
                    pair = i2 * 2 + pp
                    dve.wait_ge(a_ready, pair * U)
                    step(dve.tensor_copy(bcur[:, :], bias[:, bass.ds(pair * 2, 2)]))
                    read_out(i2, 3 * pp, qT, DH ** -0.5)
                    dve.wait_ge(w.tile_free[NT - 1], i2 * 6 + (3 * pp + 1))
                    for h2 in range(2):
                        dve.tensor_copy(qd[hr(h2), :, h2, :], qT[hr(h2), SEQ:T].rearrange("p (b t) -> p b t", t=ST))\
                            .then_inc(qd_ready, 1)
                    read_out(i2, 3 * pp + 1, kT)
                    read_out(i2, 3 * pp + 2, vT)
                    clamp(pair, 0)
                    for i in range(U):
                        if i + 1 < U:
                            clamp(pair, i + 1)
                        softplus(pair, i)
                        if i - 2 in run_end:
                            run_out(pair, run_end[i - 2])
                        if TURN <= i < TURN + SB:
                            b = i - TURN
                            dve.wait_ge(k_turned, pair * 16 + (2 * b + 2))
                            if b >= 2:
                                dve.wait_ge(zs_done, pair * SB + (b - 1))
                            dve.tensor_copy(kpT[b % 2][:, 512:1024], m.bank[1][:, :]).then_inc(kt_dve, 1)
                        if i == Z_IN:
                            dve.wait_ge(zs_done, pair * SB + SB)
                            for h2 in range(2):
                                half = slice(256 * h2, 256 * h2 + 256)
                                dve.tensor_scalar(zcs[:, half], m.bank[7][:, half], bcur[:, h2:h2 + 1], CLAMP, ALU.add,
                                                  ALU.min).then_inc(zcs_ready, 1)
                            dve.wait_ge(zs_ready, pair + 1)
                            for h2 in range(2):
                                nh = slice(NS * h2, NS * h2 + NS)
                                dve.tensor_scalar(zcn[:, nh], m.bank[2][0:NS, nh], bcur[0:NS, h2:h2 + 1], CLAMP, ALU.add,
                                                  ALU.min).then_inc(zcs_ready, 1)
                        if i == SP_OUT:
                            dve.wait_ge(lns_ready, pair * 2 + 2)
                            for h2 in range(2):
                                half, nh = slice(256 * h2, 256 * h2 + 256), slice(NS * h2, NS * h2 + NS)
                                dve.scalar_tensor_tensor(out=spn[:, nh], in0=m.bank[2][0:NS, nh], scalar=bcur[0:NS, h2:h2 + 1],
                                                         in1=zcn[:, nh], op0=ALU.add, op1=ALU.max)
                                step(dve.scalar_tensor_tensor(out=sps[:, half], in0=m.bank[7][:, half],
                                                              scalar=bcur[:, h2:h2 + 1], in1=zcs[:, half], op0=ALU.add,
                                                              op1=ALU.max))
                            dve.tensor_tensor(spn[:, :], spn[:, :], m.new01[:, :], ALU.mult).then_inc(sps_ready, 1)
                            lp, spp = by_page(laters), by_page(sps)
                            step(dve.tensor_copy(lp[:, :, NPG - 2, :], spp[:, :, NPG - 1, :]))
                            for g in range(NPG - 3, -1, -1):
                                ins = dve.tensor_tensor(lp[:, :, g, :], lp[:, :, g + 1, :], spp[:, :, g + 1, :], ALU.add)
                                if g:
                                    step(ins)
                            ins.then_inc(sps_ready, 1)
                        if i == PV0 + SB:
                            dve.wait_ge(pvs_done, pair * SB + 2 * SB)
                            for h2 in range(2):
                                ysv = y_v[hr(h2), bass.ds(pair, 1), SEQ:T].rearrange("p o (b t) -> p (o b) t", t=ST)
                                bv = m.bank[0][hr(h2), 0:64].rearrange("p (b h t) -> p b h t", h=2, t=ST)[:, :, h2, :]
                                dve.tensor_copy(ysv, bv).then_inc(ys_ok, 1)
                    run_out(pair, 3)
                step.leave(HB // 4)


def out_and_mlp(nc, m, own, w_out, w_up, w_down, gain):
    with ExitStack() as c:
        UT = 4
        CH = DFF // (UT * P)
        uhi = own.tensor("u_hi", [P, UT, T], F32R)
        ulo = own.tensor("u_lo", [P, UT, T], F32R)
        relu = [own.tensor(f"relu{t}", [P, TW], F32) for t in range(NT)]
        sqr = [own.tensor(f"relu_sq{t}", [P, TW], F32) for t in range(NT)]
        w, s = weight_sems(own.sem), norm_sems(own.sem)
        y_hi, y_x = own.sem("y_hi_ready"), own.sem("y_split")
        h_back = [own.sem(f"h_back{k}") for k in range(KT)]
        scaled, sq_ready, hi_ready, u_ready = own.sem("relu_scaled"), own.sem("relu_sq_ready"), own.sem("u_hi_ready"), own.sem("u_ready")
        out_v = w_out.rearrange("(k p) (m j) -> m p k j", p=P, j=P)
        up_v = w_up.rearrange("(k p) (c u j) -> u c p k j", p=P, j=P, u=UT)
        down_v = w_down.rearrange("(c k p) (q j) -> q c p k j", k=UT, p=P, j=2 * P)
        QD = D // (2 * P)
        stages = [(KT // 2, [(lambda i, s_=s_: out_v[i * 2 + s_], NT) for s_ in range(2)]),
                  (CH, [(lambda i, u=u: up_v[u, i], NT) for u in range(UT)]
                   + [(lambda i, q=q: down_v[q, i], 2 * NT) for q in range(QD)])]
        TILES_OUT, TILES_C = KT * NT, UT * NT + QD * 2 * NT
        USES_OUT, USES_C = KT, UT + QD * 2
        block = c.enter_context(nc.Block())

        @block.sync
        def _(sp):
            for k in range(KT):
                sp.wait_ge(y_x, k + 1)
                sp.dma_start(m.h[:, k, :], m.spill[k]).then_inc(h_back[k], 16)
            weight_loads(sp, m, w, stages)

        @block.gpsimd
        def _(pool):
            weight_splits(pool, m, w, stages)

        @block.tensor
        def _(pe):
            for n in range(KT):
                if n == 0:
                    pe.wait_ge(y_x, KT)
                dense_panel(pe, m, w, n, n % 2, n)
            pe.wait_ge(s.x, KT)
            norm_pe(pe, m, s)

            with pe.Fori(0, CH) as i:
                for u in range(UT):
                    dense_panel(pe, m, w, i * (UT + QD) + (KT + u), u % 2, i * USES_C + (USES_OUT + u))
                for q in range(QD):
                    pe.wait_ge(w.split, i * (UT + QD) + (KT + UT + q + 1))
                    for mm in range(2):
                        for t in range(NT):
                            pe.wait_ge(w.tile_free[t], i * USES_C + (USES_OUT + UT + 2 * q + mm))
                            if q == 0 and mm == 0:
                                pe.wait_ge(u_ready, i * (UT * NT) + ((UT - 1) * NT + t + 1))
                            dense_tile(pe, m.whi[q % 2], m.wlo[q % 2], UT, mm * P, uhi, ulo, t, m.bank[t])\
                                .then_inc(w.tile_ready, 1)

        @block.scalar
        def _(act):
            for k in range(KT):
                act.activation(m.xhi[:, k, :], m.h[:, k, :], ACT.Copy).then_inc(y_hi, 1)
            for t in range(NT):
                act.wait_ge(w.tile_free[t], USES_OUT)
            norm_act(act, m, s, m.h, gain)
            norm_act_rs(act, m, s)
            with act.Fori(0, CH) as i:
                for u in range(UT):
                    for t in range(NT):
                        n = u * NT + t
                        act.wait_ge(w.tile_ready, i * TILES_C + (TILES_OUT + n + 1))
                        act.activation(relu[t][:, :], m.bank[t][:, 0:TW], ACT.Relu).then_inc(w.tile_free[t], 1)
                        act.wait_ge(scaled, i * (UT * NT) + (n + 1))
                        act.activation(sqr[t][:, :], relu[t][:, :], ACT.Square).then_inc(sq_ready, 1)

        @block.vector
        def _(dve):
            for k in range(KT):
                dve.wait_ge(y_hi, k + 1)
                dve.tensor_tensor(m.xlo[:, k, :], m.h[:, k, :], f32(m.xhi[:, k, :]), ALU.subtract).then_inc(y_x, 1)
            for k in range(KT):
                dve.wait_ge(h_back[k], 16)
                for t in range(NT):
                    dve.wait_ge(w.tile_ready, k * NT + t + 1)
                    ht = m.h[:, k, t * TW:(t + 1) * TW]
                    dve.tensor_tensor(ht, m.bank[t][:, 0:TW], ht, ALU.add).then_inc(w.tile_free[t], 1)
            for t in range(NT):
                dve.wait_ge(w.tile_free[t], USES_OUT)
            norm_dve(dve, m, s, m.h, gain)
            dve.wait_ge(s.rs, 1)
            with dve.Fori(0, CH) as i:
                for u in range(UT):
                    for t in range(NT):
                        n, toks = u * NT + t, slice(t * TW, (t + 1) * TW)
                        dve.wait_ge(w.tile_free[t], i * USES_C + (USES_OUT + u + 1))
                        dve.tensor_tensor(relu[t][:, :], relu[t][:, :], m.rs[:, toks], ALU.mult).then_inc(scaled, 1)
                        dve.wait_ge(sq_ready, i * (UT * NT) + (n + 1))
                        dve.tensor_copy(uhi[:, u, toks], sqr[t][:, :]).then_inc(hi_ready, 1)
                        dve.wait_ge(hi_ready, i * (UT * NT) + (n + 1))
                        dve.tensor_tensor(ulo[:, u, toks], sqr[t][:, :], f32(uhi[:, u, toks]), ALU.subtract)\
                            .then_inc(u_ready, 1)
                for q in range(QD):
                    for mm in range(2):
                        for t in range(NT):
                            dve.wait_ge(w.tile_ready,
                                        i * TILES_C + (TILES_OUT + UT * NT + (2 * q + mm) * NT + t + 1))
                            ht = m.h[:, 2 * q + mm, t * TW:(t + 1) * TW]
                            dve.tensor_tensor(ht, m.bank[t][:, 0:TW], ht, ALU.add).then_inc(w.tile_free[t], 1)


INPUTS = ["x_prompt", "x_sample", "state_c", "state_n", "state_m", "cache_k", "cache_v", "page_table", "norm_mix",
          "norm_mlp", "w_in_a", "b_i", "b_f", "head_norm_a", "w_out_a", "norm_kv", "w_kv", "w_q_b", "w_out_b",
          "sb_bias", "w_up", "w_down", "norm_final"]
OUTPUTS = [("y_prompt", (1, SEQ, D)), ("y_sample", (SB, ST, D)),
           ("c_prompt", (1, 1, HA, DK, DV)), ("n_prompt", (1, 1, HA, DK)), ("m_prompt", (1, 1, HA)),
           ("k_prompt", (1, SEQ, HB, DH)), ("v_prompt", (1, SEQ, HB, DH)),
           ("c_sample", (1, SB, HA, DK, DV)), ("n_sample", (1, SB, HA, DK)), ("m_sample", (1, SB, HA)),
           ("k_sample", (SB, ST, HB, DH)), ("v_sample", (SB, ST, HB, DH))]


def program(nc, d):
    with ExitStack() as c:
        def sb(name, shape, dt=F32):
            return c.enter_context(nc.sbuf_tensor(name, shape, dt))

        m = Fields()
        m.d = d
        m.h = sb("h", [P, KT, T])
        m.xhi, m.xlo = sb("x_hi", [P, KT, T], F32R), sb("x_lo", [P, KT, T], F32R)
        m.wraw = [sb(f"w_raw{i}", [P, D]) for i in range(2)]
        m.whi = [sb(f"w_hi{i}", [P, D], F32R) for i in range(2)]
        m.wlo = [sb(f"w_lo{i}", [P, D], F32R) for i in range(2)]
        m.rs, m.acc = sb("rms_inverse", [P, T]), sb("squares", [P, T])
        m.sq = [sb(f"square{i}", [P, T]) for i in range(2)]
        m.ident, m.identb = sb("identity", [P, P]), sb("identity_bf16", [P, P], BF16)
        m.ones, m.negones, m.negtri = sb("ones", [P, P]), sb("minus_ones", [P, P]), sb("minus_later", [P, P])
        m.causal, m.strict, m.strict01 = sb("causal", [P, P], BF16), sb("strict", [P, P], BF16), sb("strict01", [P, P])
        m.causal_s = sb("causal_sample", [NS, NS], BF16)
        m.new_mask, m.new01 = sb("new_mask", [NS, 2 * NS], BF16), sb("new01", [NS, 2 * NS])
        m.eps = sb("eps", [P, 1])
        m.g_mix = [sb(f"g_mix{l}", [P, KT]) for l in range(2)]
        m.g_mlp = [sb(f"g_mlp{l}", [P, KT]) for l in range(2)]
        m.g_kv, m.g_final = sb("g_kv", [P, KT]), sb("g_final", [P, KT])
        m.bank = [c.enter_context(nc.psum_tensor(f"bank{i}", [P, 512], F32)) for i in range(8)]
        m.spill = nc.dram_tensor("h_spill", [KT, P, T], F32, kind="Internal").ap()
        used, done = [0], []

        def phase(f, *args):
            used[0] += 1
            with ExitStack() as stack:
                own = Own(nc, stack, used[0])
                f(nc, m, own, *args)
                done.extend(own.sems)

        with nc.Block() as block:
            @block.scalar
            def _(act):
                act.preload_act_table_set("natural_log_exp_and_others")
        phase(constants)
        phase(embed)
        phase(mixer_a)
        phase(out_and_mlp, d["w_out_a"][0], d["w_up"][0], d["w_down"][0], m.g_mlp[0])
        nc.clear_and_free_semaphores(done)
        nc.all_engine_barrier()
        phase(mixer_b)
        phase(out_and_mlp, d["w_out_b"][0], d["w_up"][1], d["w_down"][1], m.g_mlp[1])
        phase(final)


def kernel(**inputs):
    import numpy as _np
    import concourse.bacc as _bacc
    from concourse.bass_utils import run_bass_kernel_spmd as _run

    nc = _bacc.Bacc("TRN2", target_bir_lowering=False, num_devices=1)
    arrays, d = {}, {}
    for name in INPUTS:
        a = _np.ascontiguousarray(inputs[name])
        arrays[f"in_{name}"] = a
        d[name] = nc.dram_tensor(f"in_{name}", a.shape, mybir.dt.from_np(a.dtype), kind="ExternalInput").ap()
    for name, shape in OUTPUTS:
        d[name] = nc.dram_tensor(f"out_{name}", shape, F32, kind="ExternalOutput").ap()
    program(nc, d)
    r = _run(nc, [arrays], core_ids=[0])
    return tuple(r.results[0][f"out_{name}"] for name, _ in OUTPUTS)
```

```python
from contextlib import ExitStack

import concourse.bass as bass
from concourse import mybir

ALU = mybir.AluOpType
ACT = mybir.ActivationFunctionType
AX = mybir.AxisListType
F32 = mybir.dt.float32
F32R = mybir.dt.float32r
BF16 = mybir.dt.bfloat16
I32 = mybir.dt.int32

P = 128
D = 1024
KT = D // P
SEQ = 1024
SB, ST = 8, 4
NS = SB * ST
T = SEQ + NS
NT = 3
TW = T // NT
NC = SEQ // P
NB = NC + 1
HA, DK, DV = 8, 64, 128
HB, DH = 16, 64
DFF = 4096
EPS = 1e-6
PAGE, NPG = 128, 8
NEG = -1e30
FIRST = 1
CLAMP = 40.0


class Fields:
    pass


def f32(ap):
    return ap.bitcast(F32)


def blocks_of(c):
    return (c * P, P) if c < NC else (SEQ, NS)


class Own:

    def __init__(self, nc, stack, number):
        self.nc, self.stack, self.number, self.sems = nc, stack, number, []

    def sem(self, name):
        self.sems.append(self.nc.alloc_semaphore(name=f"p{self.number}_{name}"))
        return self.sems[-1]

    def tensor(self, name, shape, dt=F32):
        return self.stack.enter_context(self.nc.sbuf_tensor(f"p{self.number}_{name}", shape, dt))


class Pipe:

    def __init__(self, eng, sem):
        self.eng, self.sem, self.n, self.base = eng, sem, 0, 0

    def __call__(self, ins):
        ins.then_inc(self.sem, 1)
        self.n += 1
        self.eng.wait_ge(self.sem, self.base + self.n)

    def enter(self, i, per):
        self.start, self.per, self.base = self.n, per, i * per

    def leave(self, trips):
        assert self.n - self.start == self.per, (self.n - self.start, self.per)
        self.n, self.base = self.start + self.per * trips, 0


def weight_sems(sem):
    w = Fields()
    w.loaded = [sem("w_loaded0"), sem("w_loaded1")]
    w.hi, w.split, w.gained, w.pool_passed = sem("w_hi_ready"), sem("w_split"), sem("w_gained"), sem("w_pool_passed")
    w.tile_ready, w.tile_free = sem("tile_ready"), [sem(f"tile_free{t}") for t in range(NT)]
    return w


def weight_turns(eng, stages, panel):
    n = tiles = before = 0
    for turns, panels in stages:
        per, per_tiles = len(panels), sum(x[1] for x in panels)
        assert per % 2 == 0

        def turn(i, last, n0=n, t0=tiles, panels=panels, per=per, per_tiles=per_tiles):
            done = 0
            for j, (src, k, *gain) in enumerate(panels):
                panel(i, i * per + (n0 + j), i * (per // 2) + (n0 // 2 + j // 2), j % 2,
                      i * per_tiles + (t0 + done - last), src, *gain)
                done, last = done + k, k
        turn(0, before)
        before = panels[-1][1]
        if turns > 1:
            with eng.Fori(1, turns) as i:
                turn(i, before)
        n, tiles = n + per * turns, tiles + per_tiles * turns


def weight_loads(sp, m, w, stages, behind=None):
    def panel(i, n, in_slot, slot, tiles, src):
        if not isinstance(n, int) or n >= 2:
            sp.wait_ge(w.split, n - 1)
        ap = src(i)
        sp.dma_start(m.wraw[slot][:, :].rearrange("p (k j) -> p k j", j=ap.shape[-1]), ap)\
            .then_inc(w.loaded[slot], 16)
        if behind is not None:
            for j, entry in enumerate(stages[-1][1]):
                if entry[0] is src:
                    behind(i, j)
    weight_turns(sp, stages, panel)


def gather_page(nc, sp, m, n, cache, pages, gathered):
    page = sp.value_load(m.ptab[0:1, bass.ds(n, 1)], min_val=0, max_val=cache.shape[0] - 1)
    sp.dma_start(pages[bass.ds(n, 1)], cache[bass.ds(page, 1)]).then_inc(gathered, 16)


def weight_splits(pool, m, w, stages):
    def panel(i, n, in_slot, slot, tiles, src, gain=None):
        pool.wait_ge(w.loaded[slot], (in_slot + 1) * 16)
        if not isinstance(n, int) or n >= 2:
            pool.wait_ge(w.tile_ready, tiles)
        pool.sem_inc(w.pool_passed, 1)
        if gain is not None:
            wv = m.wraw[slot][:, :].rearrange("p (k j) -> p k j", k=KT)
            pool.tensor_tensor(wv, wv, gain[:, :].unsqueeze(2).broadcast_to([P, KT, P]), ALU.mult).then_inc(w.gained, 1)
            pool.wait_ge(w.gained, n + 1)
            pool.sem_inc(w.pool_passed, 1)
        pool.tensor_copy(m.whi[slot][:, :], m.wraw[slot][:, :]).then_inc(w.hi, 1)
        pool.wait_ge(w.hi, n + 1)
        pool.tensor_tensor(m.wlo[slot][:, :], m.wraw[slot][:, :], f32(m.whi[slot][:, :]), ALU.subtract)\
            .then_inc(w.split, 1)
    weight_turns(pool, stages, panel)


def dense_tile(pe, whi, wlo, nk, off, xhi, xlo, t, bank):
    width = 1024 // nk
    last = None
    for k in range(nk):
        wh, wl = whi[:, k * width + off:k * width + off + P], wlo[:, k * width + off:k * width + off + P]
        xh, xl = xhi[:, k, t * TW:(t + 1) * TW], xlo[:, k, t * TW:(t + 1) * TW]
        pe.matmul(bank[:, 0:TW], wh, xh, start=(k == 0), stop=False)
        pe.matmul(bank[:, 0:TW], wh, xl, start=False, stop=False)
        last = pe.matmul(bank[:, 0:TW], wl, xh, start=False, stop=(k == nk - 1))
    return last


def dense_panel(pe, m, w, n, slot, before, x_ready=None):
    pe.wait_ge(w.split, n + 1)
    for t in range(NT):
        if x_ready is not None:
            x_ready(t)
        pe.wait_ge(w.tile_free[t], before)
        dense_tile(pe, m.whi[slot], m.wlo[slot], KT, 0, m.xhi, m.xlo, t, m.bank[t]).then_inc(w.tile_ready, 1)


def dense_first(pe, m, w, n, slot, before, x):
    pe.wait_ge(w.split, n + 1)
    for t in range(NT):
        if before:
            pe.wait_ge(w.tile_free[t], before)
    for k in range(KT):
        pe.wait_ge(x, k + 1)
        for t in range(NT):
            wh, wl = m.whi[slot][:, k * P:(k + 1) * P], m.wlo[slot][:, k * P:(k + 1) * P]
            xh, xl = m.xhi[:, k, t * TW:(t + 1) * TW], m.xlo[:, k, t * TW:(t + 1) * TW]
            pe.matmul(m.bank[t][:, 0:TW], wh, xh, start=(k == 0), stop=False)
            pe.matmul(m.bank[t][:, 0:TW], wh, xl, start=False, stop=False)
            last = pe.matmul(m.bank[t][:, 0:TW], wl, xh, start=False, stop=(k == KT - 1))
            if k == KT - 1:
                last.then_inc(w.tile_ready, 1)


def norm_sems(sem):
    s = Fields()
    s.hi, s.x, s.sq, s.acc = sem("x_hi_ready"), sem("x_ready"), sem("square_ready"), sem("squares_added")
    s.sum, s.ln, s.rs = sem("sum_of_squares"), sem("rms_ln"), sem("rms_ready")
    return s


def norm_act_hi(act, m, s, h, gain):
    for k in range(KT):
        act.activation(m.xhi[:, k, :], h[:, k, :], ACT.Copy, scale=1.0 if gain is None else gain[:, k:k + 1])\
            .then_inc(s.hi, 1)


def norm_square(act, m, s, h, k):
    if k >= 2:
        act.wait_ge(s.acc, k - 1)
    act.activation(m.sq[k % 2][:, :], h[:, k, :], ACT.Square).then_inc(s.sq, 1)


def norm_act(act, m, s, h, gain):
    norm_act_hi(act, m, s, h, gain)
    for k in range(KT):
        norm_square(act, m, s, h, k)


def norm_dve_lo(dve, m, s, h, gain):
    for k in range(KT):
        dve.wait_ge(s.hi, k + 1)
        dve.scalar_tensor_tensor(out=m.xlo[:, k, :], in0=h[:, k, :], scalar=1.0 if gain is None else gain[:, k:k + 1],
                                 in1=f32(m.xhi[:, k, :]), op0=ALU.mult, op1=ALU.subtract).then_inc(s.x, 1)


def norm_add(dve, m, s, k):
    dve.wait_ge(s.sq, k + 1)
    if k == 0:
        dve.tensor_copy(m.acc[:, :], m.sq[0][:, :]).then_inc(s.acc, 1)
    else:
        dve.wait_ge(s.acc, k)
        dve.tensor_tensor(m.acc[:, :], m.acc[:, :], m.sq[k % 2][:, :], ALU.add).then_inc(s.acc, 1)


def norm_dve(dve, m, s, h, gain):
    norm_dve_lo(dve, m, s, h, gain)
    for k in range(KT):
        norm_add(dve, m, s, k)


def norm_pe(pe, m, s):
    pe.wait_ge(s.acc, KT)
    for t in range(NT):
        pe.matmul(m.bank[3 + t][:, 0:TW], m.ones[:, :], m.acc[:, t * TW:(t + 1) * TW], start=True, stop=True)\
            .then_inc(s.sum, 1)


def norm_act_rs(act, m, s):
    for t in range(NT):
        act.wait_ge(s.sum, t + 1)
        act.activation(m.rs[:, t * TW:(t + 1) * TW], m.bank[3 + t][:, 0:TW], ACT.Ln, bias=m.eps[:, 0:1],
                       scale=1.0 / D).then_inc(s.ln, 1)
    act.wait_ge(s.ln, NT)
    act.activation(m.rs[:, :], m.rs[:, :], ACT.Exp, scale=-0.5).then_inc(s.rs, 1)


def constants(nc, m, own):
    made, landed = own.sem("constants_made"), own.sem("gains_landed")
    with nc.Block() as block:
        @block.gpsimd
        def _(pool):
            pool.memset(m.ident[:, :], 0.0).then_inc(made, 1)
            pool.memset(m.identb[:, :], 0.0).then_inc(made, 1)
            pool.memset(m.ones[:, :], 1.0).then_inc(made, 1)
            pool.memset(m.negones[:, :], -1.0).then_inc(made, 1)
            pool.memset(m.negtri[:, :], -1.0).then_inc(made, 1)
            pool.memset(m.causal[:, :], 0.0).then_inc(made, 1)
            pool.memset(m.causal_s[:, :], 0.0).then_inc(made, 1)
            pool.memset(m.strict[:, :], 0.0).then_inc(made, 1)
            pool.memset(m.strict01[:, :], 1.0).then_inc(made, 1)
            pool.memset(m.new_mask[:, :], 0.0).then_inc(made, 1)
            pool.memset(m.new01[:, :], 1.0).then_inc(made, 1)
            pool.memset(m.eps[:, :], EPS).then_inc(made, 1)
            pool.wait_ge(made, 12)
            n = 12

            def keep(ap, op, fill, base, pattern, cm):
                nonlocal n
                pool.affine_select(out=ap, in_=ap, compare_op=op, fill=fill, base=base, pattern=pattern,
                                   channel_multiplier=cm).then_inc(made, 1)
                n += 1
                pool.wait_ge(made, n)

            keep(m.ident[:, :], ALU.not_equal, 1.0, 0, [[-1, P]], 1)
            keep(m.identb[:, :], ALU.not_equal, 1.0, 0, [[-1, P]], 1)
            keep(m.negtri[:, :], ALU.is_ge, 0.0, 0, [[-1, P]], 1)
            keep(m.causal[:, :], ALU.is_ge, NEG, 0, [[1, P]], -1)
            keep(m.strict[:, :], ALU.is_ge, NEG, -1, [[1, P]], -1)
            keep(m.strict01[:, :], ALU.is_ge, 0.0, -1, [[1, P]], -1)
            cs = m.causal_s[:, :].rearrange("s (b t) -> s b t", b=SB)
            keep(cs, ALU.is_ge, NEG, 0, [[ST, SB], [1, ST]], -1)
            keep(cs, ALU.is_ge, NEG, 0, [[-ST, SB], [0, ST]], 1)
            for tile, fill in ((m.new_mask, NEG), (m.new01, 0.0)):
                v = tile[:, :].rearrange("s (h b t) -> s h b t", h=2, b=SB)
                keep(v, ALU.is_ge, fill, -1, [[0, 2], [ST, SB], [1, ST]], -1)
                keep(v, ALU.is_ge, fill, 0, [[0, 2], [-ST, SB], [0, ST]], 1)

        @block.sync
        def _(sp):
            gains = [(m.g_mix[l], m.d["norm_mix"][l]) for l in range(2)]
            gains += [(m.g_mlp[l], m.d["norm_mlp"][l]) for l in range(2)]
            gains += [(m.g_kv, m.d["norm_kv"])]
            with nc.allow_non_contiguous_dma(reason="five gains of 4 KB, a feature to a partition"):
                for tile, src in gains:
                    sp.dma_start(tile[:, :], src.rearrange("(k p) -> p k", p=P)).then_inc(landed, 16)
            sp.dma_start(m.ptab[:, :], m.d["page_table"].rearrange("b (o g) -> o (b g)", o=1)).then_inc(landed, 16)
            sp.wait_ge(landed, 16 * len(gains) + 16)


def embed(nc, m, own):
    with ExitStack() as c:
        xin = own.tensor("x_rows", [P, NB, D], F32)
        landed = [own.sem(f"x_landed{b}") for b in range(NB)]
        turned, free_dve, free_act = own.sem("x_turned"), own.sem("x_bank_free_dve"), own.sem("x_bank_free_act")
        block = c.enter_context(nc.Block())

        @block.sync
        def _(sp):
            for b in range(NB):
                t0, n = blocks_of(b)
                src = m.d["x_prompt"][0, t0:t0 + n, :] if b < NC else m.d["x_sample"].rearrange("b t d -> (b t) d")
                sp.dma_start(xin[0:n, b, :], src).then_inc(landed[b], 16)

        @block.tensor
        def _(pe):
            g = 0
            for b in range(NB):
                n = blocks_of(b)[1]
                pe.wait_ge(landed[b], 16)
                for half in range(2):
                    if g >= 4:
                        pe.wait_ge(free_act if g % 2 else free_dve, (g - 4) // 2 + 1)
                    for q in range(4):
                        k = 4 * half + q
                        last = pe.transpose(m.bank[g % 4][:, q * P:q * P + n], xin[0:n, b, k * P:(k + 1) * P],
                                            m.ident[0:n, 0:n])
                    last.then_inc(turned, 1)
                    g += 1

        def read_out(eng, op, which, free):
            for g in range(which, 2 * NB, 2):
                t0, n = blocks_of(g // 2)
                eng.wait_ge(turned, g + 1)
                src = m.bank[g % 4][:, :].rearrange("p (q t) -> p q t", q=4)[:, :, 0:n]
                op(m.h[:, 4 * (g % 2):4 * (g % 2) + 4, t0:t0 + n], src).then_inc(free, 1)

        @block.vector
        def _(dve):
            read_out(dve, dve.tensor_copy, 0, free_dve)

        @block.scalar
        def _(act):
            read_out(act, act.copy, 1, free_act)


def final(nc, m, own):
    SLOTS = 3
    with ExitStack() as c:
        rows = [own.tensor(f"y_rows{i}", [P, D]) for i in range(SLOTS)]
        gain = own.tensor("gain_rows", [P, D])
        junk = [own.tensor(f"squares{i}", [P, 512]) for i in range(2)]
        part, rs = own.tensor("half_sums", [P, NB, 2]), own.tensor("row_rms", [P, NB])
        gain_in, turned, squared, summed = own.sem("gain_in"), own.sem("y_turned"), own.sem("squared"), own.sem("summed")
        ln, rs_ready, scaled = own.sem("row_ln"), own.sem("row_rms_ready"), own.sem("y_scaled")
        stored = [own.sem(f"y_stored{i}") for i in range(SLOTS)]
        block = c.enter_context(nc.Block())

        @block.tensor
        def _(pe):
            for g in range(2 * NB):
                t0, n = blocks_of(g // 2)
                if g >= 8:
                    pe.wait_ge(scaled, g - 7)
                for q in range(4):
                    last = pe.transpose(m.bank[g % 8][0:n, q * P:(q + 1) * P], m.h[:, 4 * (g % 2) + q, t0:t0 + n],
                                        m.ident[:, :])
                last.then_inc(turned, 1)

        @block.scalar
        def _(act):
            def rms(b):
                n = blocks_of(b)[1]
                act.wait_ge(summed, b + 1)
                act.activation(rs[0:n, b:b + 1], part[0:n, b, 0:1], ACT.Ln, bias=m.eps[0:n, 0:1], scale=1.0 / D).then_inc(ln, 1)
                act.wait_ge(ln, b + 1)
                act.activation(rs[0:n, b:b + 1], rs[0:n, b:b + 1], ACT.Exp, scale=-0.5).then_inc(rs_ready, 1)

            for g in range(2 * NB):
                n = blocks_of(g // 2)[1]
                act.wait_ge(turned, g + 1)
                if g >= 2:
                    act.wait_ge(squared, g - 1)
                act.activation(junk[g % 2][0:n, :], m.bank[g % 8][0:n, :], ACT.Square,
                               accum_out=part[0:n, g // 2, g % 2:g % 2 + 1]).then_inc(squared, 1)
                if g % 2 and g > 1:
                    rms(g // 2 - 1)
            rms(NB - 1)

        @block.vector
        def _(dve):
            dve.wait_ge(gain_in, 16)

            def scale(b):
                n = blocks_of(b)[1]
                dve.wait_ge(rs_ready, b + 1)
                if b >= SLOTS:
                    dve.wait_ge(stored[b % SLOTS], 16 * (b // SLOTS))
                for half in range(2):
                    cols = slice(512 * half, 512 * half + 512)
                    dve.scalar_tensor_tensor(out=rows[b % SLOTS][0:n, cols], in0=m.bank[(2 * b + half) % 8][0:n, :],
                                             scalar=rs[0:n, b:b + 1], in1=gain[0:n, cols], op0=ALU.mult, op1=ALU.mult)\
                        .then_inc(scaled, 1)

            for b in range(NB):
                n = blocks_of(b)[1]
                dve.wait_ge(squared, 2 * b + 2)
                dve.tensor_tensor(part[0:n, b, 0:1], part[0:n, b, 0:1], part[0:n, b, 1:2], ALU.add).then_inc(summed, 1)
                if b:
                    scale(b - 1)
            scale(NB - 1)

        @block.sync
        def _(sp):
            sp.dma_start(gain[:, :], m.d["norm_final"].rearrange("(o f) -> o f", o=1).broadcast_to([P, D])).then_inc(gain_in, 16)
            for b in range(NB):
                t0, n = blocks_of(b)
                dst = m.d["y_prompt"][0, t0:t0 + n, :] if b < NC else m.d["y_sample"].rearrange("b t d -> (b t) d")
                sp.wait_ge(scaled, 2 * b + 2)
                sp.dma_start(dst, rows[b % SLOTS][0:n, :]).then_inc(stored[b % SLOTS], 16)
            for i in range(SLOTS):
                sp.wait_ge(stored[i], 16 * len(range(i, NB, SLOTS)))


def mixer_a(nc, m, own):
    HP = HA // 2
    GROUPS = [(0, 4), (4, 4), (8, 1)]
    OUT_GROUPS = [(0, 4), (8, 1), (4, 4)]
    DA = DV + 1
    with ExitStack() as c:
        sb = own.tensor

        qT, kT = sb("q_t", [P, T]), sb("k_t", [P, T])
        qst, kst, vst = sb("q_next", [P, T]), sb("k_next", [P, T]), [sb(f"v_next{i}", [P, T]) for i in range(2)]
        ktok, vtok = sb("k_rows", [P, NB, P]), sb("v_rows", [P, NB, 2, DA])
        dec, num = sb("decay_weights", [P, T]), sb("numerator", [P, NB, DA])
        C, Cs = sb("state", [P, DA]), sb("state_sample", [P, SB, DA])
        qsel = sb("q_by_sequence", [P, SB * (NS + ST)])
        tokg = sb("gate_columns", [P, NB, 96])
        wt = [sb(f"scores{i}", [P, P]) for i in range(2)]
        kw = [sb(f"k_weighted{i}", [P, DK]) for i in range(2)]
        kws, inter = sb("k_weighted_sample", [NS, SB, DK]), sb("inter", [P, DA])
        sqj, ss, den = sb("square_junk", [P, DV]), sb("head_squares", [P, NB]), sb("denominator", [P, NB])
        pick = sb("pick_gates", [P, P])
        gbias, m0, mprev, mend = sb("gate_bias", [40, 1]), sb("m_start", [HA, SB]), sb("m_prev", [HA, 16]), sb("m_end", [HA, 16])
        wend, wdiag, decb = sb("w_end", [HA, 16]), sb("w_diag", [HA, HA, 16]), sb("decay_all", [P, HA, 16])
        ghead = sb("g_head", [P, HA])
        gcur, dcur, ghcur, selcur = sb("gates_now", [P, NB, 3, 2]), sb("decay_now", [P, 16]), sb("g_head_now", [P, 2]), sb("head_now", [HA, 2])
        graw, y, ub, uh = m.sq[0], m.sq[1], m.acc, m.sq[0]
        ig, bsum, mt, stack, reset = num[:, :, :].rearrange("p c e -> p (c e)")[0:HA, 0:T], kT, qT, dec, vst[0][0:HA, :]

        w, s = weight_sems(own.sem), norm_sems(own.sem)
        filled, landed = own.sem("fills"), own.sem("a_landed")
        spilled = own.sem("h_spilled")
        chain, achain = own.sem("dve_step"), own.sem("act_step")
        picked = own.sem("gates_picked")
        y_ready, sp_ready, m_ready, we_in, stack_act = own.sem("softplus_in"), own.sem("softplus_out"), own.sem("m_ready"), own.sem("w_inter_in"), own.sem("stack_act")
        stacked, col_turned, col_ready = own.sem("stack_ready"), own.sem("columns_turned"), own.sem("columns_ready")
        diag_ready, decb_turned = own.sem("w_diag_ready"), own.sem("decay_spread")
        in_turned, in_ready = own.sem("rows_turned"), own.sem("rows_ready")
        qsel_ready, o_exp = own.sem("q_by_sequence_ready"), own.sem("o_exp")
        uh_ready, u_spread, d_ready = own.sem("u_head_ready"), own.sem("u_spread"), own.sem("decay_ready")
        s_ready, wt_ready, kw_ready = own.sem("scores_ready"), own.sem("weighted_ready"), own.sem("kw_ready")
        n1_ready, n2_ready, n2_scaled, num_ready = own.sem("intra_ready"), own.sem("inter_ready"), own.sem("inter_scaled"), own.sem("num_ready")
        dc_ready, c_ready = own.sem("state_add_ready"), own.sem("state_ready")
        dcs_ready, cs_ready = own.sem("state_s_add_ready"), own.sem("state_s_ready")
        h_ready, sq_sum, r_ready, hn_ready = own.sem("head_out"), own.sem("head_squares_ready"), own.sem("head_rms"), own.sem("head_normed")
        out_turned, y_ok = own.sem("head_turned"), own.sem("y_tile")
        state_in, state_out, m_stored = own.sem("state_loaded"), own.sem("state_stored"), own.sem("m_stored")

        win = m.d["w_in_a"][0]
        win_v = win[:, 0:3072].rearrange("(k p) (m j) -> m p k j", p=P, j=P)
        last128 = win[:, 3088 - P:3088].rearrange("(k p) j -> p k j", p=P)
        stages = [(1, [(lambda i: last128, NT), (lambda i: last128, 0)]),
                  (HP, [(lambda i: win_v[i], NT), (lambda i: win_v[i + 4], NT),
                        (lambda i: win_v[i * 2 + 8], NT), (lambda i: win_v[i * 2 + 16], NT),
                        (lambda i: win_v[i * 2 + 9], NT), (lambda i: win_v[i * 2 + 17], NT)])]
        cs_d = m.d["state_c"][0].rearrange("b (p h) k v -> p (h k) b v", h=2)
        ns_d = m.d["state_n"][0].rearrange("b (p h) k -> p (h k) b", h=2)
        cso_d = m.d["c_sample"][0].rearrange("b (p h) k v -> p (h k) b v", h=2)
        nso_d = m.d["n_sample"][0].rearrange("b (p h) k -> p (h k) b", h=2)
        cp_d = m.d["c_prompt"][0, 0].rearrange("(p h) k v -> p (h k) v", h=2)
        np_d = m.d["n_prompt"][0, 0].rearrange("(p h) k -> p (h k)", h=2)
        y_v = m.h[:, :, :].rearrange("p (q h) t -> p q h t", h=2)
        gathered = own.sem("pages_gathered")
        pe_passed, dve_passed, qk_ready = own.sem("pe_passed"), own.sem("dve_passed"), own.sem("q_and_k_taken")
        BEHIND, AHEAD = ((0, 1, 2, 3, 4, 5), (1, 3, 5)), (9, 6)
        TILES, FIRST_TILES = 6 * NT, 9

        def gate_of(p, h2, ts=slice(0, T)):
            return y_v[:, bass.ds(p, 1), h2, ts].rearrange("p q t -> p (q t)")
        block = c.enter_context(nc.Block())

        @block.sync
        def _(sp):
            with nc.allow_non_contiguous_dma(reason="gate biases, head gains and stabilisers, 4 KB in all"):
                sp.dma_start(gbias[0:HA, :], m.d["b_i"].rearrange("l h -> h l")).then_inc(landed, 16)
                sp.dma_start(gbias[32:40, :], m.d["b_f"].rearrange("l h -> h l")).then_inc(landed, 16)
                sp.dma_start(m0[:, :], m.d["state_m"][0].rearrange("b h -> h b")).then_inc(landed, 16)
                sp.dma_start(ghead[:, :], m.d["head_norm_a"][0].rearrange("h e -> e h")).then_inc(landed, 16)
            def behind(i, j):
                if j < 4:
                    for x in range(4):
                        gather_page(nc, sp, m, i * 16 + (4 * j + x), m.d["cache_k"], m.k_pages, gathered)
            weight_loads(sp, m, w, stages, behind)
            sp.wait_ge(gathered, 16 * SB * NPG)

        def act_side_loads(act):
            for k in range(KT):
                act.dma_start(m.spill[k], m.h[:, k, :]).then_inc(spilled, 16)

        @block.gpsimd
        def _(pool):
            pool.memset(pick[:, :], 0.0).then_inc(filled, 1)
            pool.memset(stack[:, :], 0.0).then_inc(filled, 1)
            pool.memset(reset[:, :], 1.0).then_inc(filled, 1)
            pool.memset(tokg[:, :, :], 1.0).then_inc(filled, 1)
            pool.memset(vtok[:, :, :, :], 1.0).then_inc(filled, 1)
            pool.memset(qsel[:, :], 0.0).then_inc(filled, 1)
            pool.memset(ss[:, :], 1.0).then_inc(filled, 1)
            pool.wait_ge(filled, 7)
            pool.memset(reset[:, 0:SEQ].rearrange("h (c t) -> h c t", t=P)[:, :, 0:1], 0.0).then_inc(filled, 1)
            pool.memset(reset[:, SEQ:T].rearrange("h (b t) -> h b t", t=ST)[:, :, 0:1], 0.0).then_inc(filled, 1)
            pool.affine_select(out=pick[:, 0:HA], in_=pick[:, 0:HA], compare_op=ALU.not_equal, fill=1.0, base=-112,
                               pattern=[[-1, HA]], channel_multiplier=1).then_inc(filled, 1)
            pool.affine_select(out=pick[:, 32:40], in_=pick[:, 32:40], compare_op=ALU.not_equal, fill=1.0, base=-120,
                               pattern=[[-1, HA]], channel_multiplier=1).then_inc(filled, 1)
            weight_splits(pool, m, w, stages)

        def hr(h2):
            return slice(h2 * DK, (h2 + 1) * DK)

        def toks(cb):
            t0, n = blocks_of(cb)
            return slice(t0, t0 + n)

        @block.tensor
        def _(pe):
            for count in (n1_ready, dc_ready, dcs_ready, u_spread):
                pe.sem_inc(count, FIRST)
            def turn_in(p, g0, tile):
                for g, (b0, nb) in enumerate(GROUPS):
                    g += g0
                    pe.wait_ge(in_ready, FIRST + p * 9 + (g if g == 0 else g - 1))
                    if g < 2:
                        pe.wait_ge(y_ok, FIRST + p * 6)
                    for j in range(nb):
                        t0, n = blocks_of(b0 + j)
                        last = pe.transpose(m.bank[3 + g % 2][0:n, j * P:(j + 1) * P], tile[:, t0:t0 + n], m.ident[:, :])
                    last.then_inc(in_turned, 1)

            def alone():
                pe.sem_inc(pe_passed, 1)

            def tile_of(p, e, ahead=1):
                j, t = e // NT, e % NT
                pe.wait_ge(w.split, p * 6 + (6 * ahead + 3 + j))
                pe.wait_ge(w.tile_free[t], p * 6 + (6 * ahead + 1 + j))
                dense_tile(pe, m.whi[j % 2], m.wlo[j % 2], KT, 0, m.xhi, m.xlo, t, m.bank[t]).then_inc(w.tile_ready, 1)

            def spread(p, h2, j):
                hh = p * 2 + h2
                t0, n = ((0, 512), (512, 512), (SEQ, NS))[j]
                if j == 0:
                    pe.wait_ge(uh_ready, hh + 1)
                pe.wait_ge(d_ready, FIRST + hh * 3 + j)
                pe.matmul(m.bank[5][:, 0:n], m.ones[0:HA, :], uh[0:HA, t0:t0 + n], start=True, stop=False)
                if j < 2:
                    last = pe.matmul(m.bank[5][:, :], m.identb[:, :], m.causal[:, :].unsqueeze(1).broadcast_to([P, 4, P]),
                                     start=False, stop=True)
                else:
                    last = pe.matmul(m.bank[5][:, 0:NS], m.identb[0:NS, :], m.causal_s[:, :], start=False, stop=True)
                last.then_inc(u_spread, 1)

            def head(p, h2, more):
                hh = p * 2 + h2
                if h2 == 0:
                    for j in range(3):
                        spread(p, 0, j)

                def scores(cb):
                    n = blocks_of(cb)[1]
                    pe.wait_ge(wt_ready, FIRST + hh * NB + cb)
                    if cb == NC:
                        alone()
                    pe.matmul(m.bank[6][0:n, 0:n], kT[hr(h2), toks(cb)], qT[hr(h2), toks(cb)], start=True, stop=True)\
                        .then_inc(s_ready, 1)

                scores(0)
                for cb in range(NB):
                    t0, n = blocks_of(cb)
                    u = hh * NB + cb
                    if cb < NC:
                        scores(cb + 1)
                    pe.wait_ge(y_ok, FIRST + hh * 3)
                    pe.wait_ge(n2_scaled, FIRST + u)
                    if cb < NC:
                        pe.wait_ge(c_ready, p * 17 + (h2 * NC + cb + 1))
                        pe.matmul(m.bank[3][0:n, 0:DA], qT[hr(h2), toks(cb)], C[hr(h2), :], start=True, stop=True)\
                            .then_inc(n2_ready, 1)
                    else:
                        pe.wait_ge(state_in, p * 32 + 32)
                        pe.wait_ge(qsel_ready, p + 1)
                        alone()
                        for b in range(SB):
                            last = pe.matmul(m.bank[3][0:n, 0:DA], qsel[hr(h2), b * NS:(b + 1) * NS], Cs[hr(h2), b, :],
                                             start=(b == 0), stop=(b == SB - 1))
                        last.then_inc(n2_ready, 1)
                    pe.wait_ge(num_ready, FIRST + u)
                    pe.wait_ge(wt_ready, FIRST + u + 1)
                    if cb == NC:
                        alone()
                    pe.matmul(m.bank[7][0:n, 0:DA], wt[cb % 2][0:n, 0:n], vtok[0:n, cb, h2, :], start=True, stop=True)\
                        .then_inc(n1_ready, 1)
                    if cb < NC:
                        pe.wait_ge(kw_ready, u + 1)
                        pe.matmul(m.bank[4][hr(h2), 0:DA], kw[cb % 2][:, :], vtok[:, cb, h2, :], start=True, stop=True)\
                            .then_inc(dc_ready, 1)
                    else:
                        pe.wait_ge(kw_ready, u + 1)
                        pe.wait_ge(c_ready, p * 17 + (h2 * NC + NC + 1))
                    if more and cb in BEHIND[h2]:
                        tile_of(p, h2 * AHEAD[0] + BEHIND[h2].index(cb))
                for g in range(3):
                    pe.wait_ge(cs_ready, FIRST + hh * 3 + g)
                    for b in range(3 * g, min(3 * g + 3, SB)):
                        last = pe.matmul(m.bank[4][hr(h2), (b % 3) * DA:(b % 3 + 1) * DA], kws[:, b, :],
                                         vtok[0:NS, NC, h2, :], start=True, stop=True)
                    last.then_inc(dcs_ready, 1)
                    if h2 == 0:
                        spread(p, 1, g)
                    if more:
                        tile_of(p, h2 * AHEAD[0] + len(BEHIND[h2]) + g)
                pe.wait_ge(hn_ready, hh + 1)
                pe.wait_ge(cs_ready, FIRST + hh * 3 + 3)
                for g, (b0, nb) in enumerate(OUT_GROUPS):
                    if g == 2:
                        pe.wait_ge(y_ok, FIRST + hh * 3 + 1)
                    for j in range(nb):
                        n = blocks_of(b0 + j)[1]
                        last = pe.transpose(m.bank[3 + g % 2][:, j * P:j * P + n], num[0:n, b0 + j, 0:DV], m.ident[0:n, 0:n])
                    last.then_inc(out_turned, 1)

            dense_first(pe, m, w, 0, 0, 0, s.x)
            norm_pe(pe, m, s)
            for t in range(NT):
                pe.wait_ge(w.tile_free[t], 1)
            pe.wait_ge(filled, 11)
            pe.wait_ge(s.rs, 1)
            for t in range(NT):
                pe.matmul(m.bank[3 + t][:, 0:TW], pick[:, :], graw[:, t * TW:(t + 1) * TW], start=True, stop=True)\
                    .then_inc(picked, 1)
            for e in range(FIRST_TILES):
                tile_of(0, e, 0)
            pe.wait_ge(stacked, 1)
            for g, (b0, nb) in enumerate(GROUPS):
                for j in range(nb):
                    t0, n = blocks_of(b0 + j)
                    last = pe.transpose(m.bank[3 + g][0:n, j * P:(j + 1) * P], stack[:, t0:t0 + n], m.ident[:, :])
                last.then_inc(col_turned, 1)
            pe.wait_ge(diag_ready, 1)
            pe.matmul(m.bank[6][:, 0:P], m.ones[0:HA, :], wdiag[:, :, :].rearrange("h g e -> h (g e)"), start=True,
                      stop=True).then_inc(decb_turned, 1)
            pe.wait_ge(col_ready, 4)
            for e in range(FIRST_TILES, sum(AHEAD)):
                tile_of(0, e, 0)

            def pair(p, more):
                for t in range(NT):
                    pe.wait_ge(w.tile_free[t], p * 6 + 6)
                for x, src in enumerate((kst, vst[0], vst[1])):
                    turn_in(p, 3 * x, src)
                    tile_of(p, sum(AHEAD) + x, 0)
                pe.wait_ge(in_ready, FIRST + p * 9 + 9)
                pe.wait_ge(qk_ready, p * 2 + 2)
                head(p, 0, more)
                head(p, 1, more)

            with pe.Fori(0, HP - 1) as p:
                pair(p, True)
            pair(HP - 1, False)

        @block.scalar
        def _(act):
            for count in (state_out, d_ready, n2_scaled, in_ready):
                act.sem_inc(count, FIRST)
            norm_act(act, m, s, m.h, m.g_mix[0])
            act_side_loads(act)
            norm_act_rs(act, m, s)
            step = Pipe(act, achain)
            act.wait_ge(y_ready, 1)
            step(act.activation(bsum[0:HA, :], bsum[0:HA, :], ACT.Exp))
            act.activation(bsum[0:HA, :], bsum[0:HA, :], ACT.Ln, bias=1.0).then_inc(sp_ready, 1)
            act.wait_ge(m_ready, 1)
            act.activation(stack[64:64 + HA, :], mt[0:HA, :], ACT.Exp, scale=-1.0).then_inc(stack_act, 1)
            act.wait_ge(we_in, 1)
            act.activation(stack[32:32 + HA, :], bsum[0:HA, :], ACT.Exp).then_inc(stack_act, 1)
            for g, (b0, nb) in enumerate(GROUPS):
                n = P if g < 2 else NS
                act.wait_ge(col_turned, g + 1)
                act.copy(tokg[0:n, b0:b0 + nb, :],
                         m.bank[3 + g][0:n, :].rearrange("p (j e) -> p j e", e=P)[:, 0:nb, 0:96]).then_inc(col_ready, 1)
            act.wait_ge(decb_turned, 1)
            act.copy(decb[:, :, :].rearrange("p h e -> p (h e)"), m.bank[6][:, 0:P]).then_inc(col_ready, 1)

            def rows(p, g0):
                for g, (b0, nb) in enumerate(GROUPS):
                    n = P if g < 2 else NS
                    g += g0
                    act.wait_ge(in_turned, p * 9 + (g + 1))
                    src = m.bank[3 + g % 2][0:n, :].rearrange("p (j e) -> p j e", e=P)[:, 0:nb, :]
                    dst = ktok[0:n, b0:b0 + nb, :] if g0 == 0 else vtok[0:n, b0:b0 + nb, g0 // 3 - 1, 0:DV]
                    act.copy(dst, src).then_inc(in_ready, 1)

            def pair(p):
                act.wait_ge(state_out, FIRST + p * 64)
                with nc.allow_non_contiguous_dma(reason="normalisers of the states"):
                    act.dma_start(Cs[:, :, 0:DV], cs_d[p]).then_inc(state_in, 16)
                    act.dma_start(Cs[:, :, DV:DA].rearrange("p b o -> p (b o)"), ns_d[p]).then_inc(state_in, 16)
                rows(p, 0)
                rows(p, 3)
                rows(p, 6)
                for i in range(2):
                    for t in range(NT):
                        act.wait_ge(w.tile_free[t], p * 6 + 7)
                    act.activation(gate_of(p, i), gate_of(p, i), ACT.Exp, scale=-1.0).then_inc(o_exp, 1)
                def decay(h2):
                    hh = p * 2 + h2
                    for j in range(3):
                        act.wait_ge(u_spread, FIRST + hh * 3 + (j + 1))
                        for cb in (range(4 * j, 4 * j + 4) if j < 2 else (NC,)):
                            t0, n = blocks_of(cb)
                            q = (cb % 4) * P
                            last = act.activation(dec[0:n, t0:t0 + n], m.bank[5][0:n, q:q + n], ACT.Exp,
                                                  bias=gcur[0:n, cb, 0, h2:h2 + 1])
                        last.then_inc(d_ready, 1)

                decay(0)
                for h2 in range(2):
                    hh = p * 2 + h2
                    for cb in range(NB):
                        n = blocks_of(cb)[1]
                        act.wait_ge(n2_ready, hh * NB + (cb + 1))
                        act.wait_ge(num_ready, FIRST + hh * NB + cb)
                        act.activation(inter[0:n, :], m.bank[3][0:n, 0:DA], ACT.Copy, scale=gcur[0:n, cb, 1, h2:h2 + 1])\
                            .then_inc(n2_scaled, 1)
                    if h2 == 0:
                        decay(1)
                    act.wait_ge(h_ready, hh + 1)
                    for cb in range(NB):
                        n = blocks_of(cb)[1]
                        act.activation(sqj[0:n, :], num[0:n, cb, 0:DV], ACT.Square, accum_out=ss[0:n, cb:cb + 1])\
                            .then_inc(sq_sum, 1)
                        act.wait_ge(sq_sum, hh * NB + (cb + 1))
                    act.activation(ss[:, :], ss[:, :], ACT.Ln, bias=m.eps[:, 0:1], scale=1.0 / DV).then_inc(r_ready, 1)
                    act.wait_ge(r_ready, hh * 2 + 1)
                    act.activation(ss[:, :], ss[:, :], ACT.Exp, scale=-0.5).then_inc(r_ready, 1)
                act.wait_ge(cs_ready, FIRST + p * 6 + 6)
                act.wait_ge(c_ready, p * 17 + 17)
                with nc.allow_non_contiguous_dma(reason="normalisers of the states"):
                    act.dma_start(cp_d[p], C[:, 0:DV]).then_inc(state_out, 16)
                    act.dma_start(np_d[p].rearrange("(q o) -> q o", o=1), C[:, DV:DA]).then_inc(state_out, 16)
                    act.dma_start(cso_d[p], Cs[:, :, 0:DV]).then_inc(state_out, 16)
                    act.dma_start(nso_d[p], Cs[:, :, DV:DA].rearrange("p b o -> p (b o)")).then_inc(state_out, 16)
            with act.Fori(0, HP) as p:
                pair(p)
            act.wait_ge(state_out, FIRST + 64 * HP)
            act.dma_start(m.d["m_prompt"][0].rearrange("o h -> h o"), mend[:, NC - 1:NC]).then_inc(m_stored, 16)
            with nc.allow_non_contiguous_dma(reason="256 bytes"):
                act.dma_start(m.d["m_sample"][0].rearrange("b h -> h b"), mend[:, NC:16]).then_inc(m_stored, 16)
            act.wait_ge(m_stored, 32)
            act.wait_ge(spilled, 16 * KT)

        @block.vector
        def _(dve):
            for count in (num_ready, y_ok, cs_ready, wt_ready):
                dve.sem_inc(count, FIRST)
            norm_dve(dve, m, s, m.h, m.g_mix[0])
            step = Pipe(dve, chain)

            def read_out(p, e, q=None):
                j, t = e // NT, e % NT
                ts = slice(t * TW, (t + 1) * TW)
                dve.wait_ge(w.tile_ready, p * 18 + (e + 4 + (18 if q else 0)))
                if j in (3, 5):
                    dst = gate_of(p + 1 if q else p, j // 4, ts)
                else:
                    dst = (qst, kst, vst[0], None, vst[1])[j][:, ts]
                if j == 1:
                    ins = dve.scalar_tensor_tensor(out=dst, in0=m.bank[t][:, 0:TW], scalar=DK ** -0.5, in1=m.rs[:, ts],
                                                   op0=ALU.mult, op1=ALU.mult)
                else:
                    ins = dve.tensor_tensor(dst, m.bank[t][:, 0:TW], m.rs[:, ts], ALU.mult)
                ins.then_inc(w.tile_free[t], 1)

            dve.wait_ge(s.rs, 1)
            for t in range(NT):
                ts = slice(t * TW, (t + 1) * TW)
                dve.wait_ge(w.tile_ready, t + 1)
                ins = dve.tensor_tensor(graw[:, ts], m.bank[t][:, 0:TW], m.rs[:, ts], ALU.mult)
                ins.then_inc(w.tile_free[t], 1)
            dve.wait_ge(landed, 64)
            dve.wait_ge(filled, 11)
            dve.wait_ge(picked, NT)
            for t in range(NT):
                ts = slice(t * TW, (t + 1) * TW)
                dve.tensor_scalar(ig[:, ts], m.bank[3 + t][0:HA, 0:TW], gbias[0:HA, 0:1], None, ALU.add)
                step(dve.tensor_scalar(y[0:HA, ts], m.bank[3 + t][32:32 + HA, 0:TW], gbias[32:32 + HA, 0:1], -1.0,
                                       ALU.add, ALU.mult))
            dve.tensor_scalar(bsum[0:HA, :], y[0:HA, :], CLAMP, None, ALU.min).then_inc(y_ready, 1)
            read_out(0, 0)
            dve.wait_ge(sp_ready, 1)
            step(dve.tensor_tensor(y[0:HA, :], y[0:HA, :], bsum[0:HA, :], ALU.max))
            step(dve.tensor_scalar(y[0:HA, :], y[0:HA, :], -1.0, None, ALU.mult))
            read_out(0, 1)
            step(dve.tensor_tensor_scan(bsum[0:HA, :], reset[:, :], y[0:HA, :], 0.0, ALU.mult, ALU.add))
            read_out(0, 2)
            step(dve.tensor_tensor_scan(mt[0:HA, 0:SEQ], y[0:HA, 0:SEQ], ig[:, 0:SEQ], 0.0, ALU.add, ALU.max))
            for b in range(SB):
                bt = slice(SEQ + b * ST, SEQ + (b + 1) * ST)
                last = dve.tensor_tensor_scan(mt[0:HA, bt], y[0:HA, bt], ig[:, bt], m0[:, b:b + 1], ALU.add, ALU.max)
            last.then_inc(m_ready, 1)
            read_out(0, 3)
            dve.wait_ge(m_ready, 1)

            def ends(ap):
                return (ap[:, 0:SEQ].rearrange("h (c t) -> h c t", t=P)[:, :, P - 1],
                        ap[:, SEQ:T].rearrange("h (b t) -> h b t", t=ST)[:, :, ST - 1])

            a, b_ = ends(mt[0:HA, :])
            dve.tensor_copy(mend[:, 0:NC], a)
            step(dve.tensor_copy(mend[:, NC:16], b_))
            dve.memset(mprev[:, 0:1], 0.0)
            dve.tensor_copy(mprev[:, 1:NC], mend[:, 0:NC - 1])
            dve.tensor_copy(mprev[:, NC:16], m0[:, :])
            dve.tensor_tensor(stack[0:HA, :], ig[:, :], bsum[0:HA, :], ALU.subtract)
            step(dve.tensor_tensor(ub[0:HA, :], bsum[0:HA, :], mt[0:HA, :], ALU.subtract))
            read_out(0, 4)
            dve.tensor_tensor(bsum[0:HA, 0:SEQ].rearrange("h (c t) -> h c t", t=P),
                              ub[0:HA, 0:SEQ].rearrange("h (c t) -> h c t", t=P),
                              mprev[:, 0:NC].unsqueeze(2).broadcast_to([HA, NC, P]), ALU.add)
            dve.tensor_tensor(bsum[0:HA, SEQ:T].rearrange("h (c t) -> h c t", t=ST),
                              ub[0:HA, SEQ:T].rearrange("h (c t) -> h c t", t=ST),
                              mprev[:, NC:16].unsqueeze(2).broadcast_to([HA, SB, ST]), ALU.add).then_inc(we_in, 1)
            read_out(0, 5)
            dve.wait_ge(stack_act, 2)
            a, b_ = ends(stack[32:32 + HA, :])
            dve.tensor_copy(wend[:, 0:NC], a).then_inc(stacked, 1)
            step(dve.tensor_copy(wend[:, NC:16], b_))
            dve.tensor_tensor(wdiag[:, :, :], wend[:, :].unsqueeze(1).broadcast_to([HA, HA, 16]),
                              m.ident[0:HA, 0:HA].unsqueeze(2).broadcast_to([HA, HA, 16]), ALU.mult).then_inc(diag_ready, 1)
            step(dve.memset(num[:, :, :], 0.0))
            for e in range(6, FIRST_TILES):
                read_out(0, e)
            dve.wait_ge(col_ready, 4)

            def post(p, h2, more):
                hh = p * 2 + h2
                step(dve.scalar_tensor_tensor(out=den[:, :], in0=num[:, :, DV], scalar=-1.0, in1=num[:, :, DV],
                                              op0=ALU.mult, op1=ALU.max))
                step(dve.tensor_tensor(den[:, :], den[:, :], gcur[:, :, 2, h2], ALU.max))
                step(dve.reciprocal(den[:, :], den[:, :]))
                hv = num[:, :, 0:DV]
                dve.tensor_tensor(hv, hv, den[:, :].unsqueeze(2).broadcast_to([P, NB, DV]), ALU.mult).then_inc(h_ready, 1)
                if more:
                    for e in range(len(BEHIND[h2]), AHEAD[h2]):
                        read_out(p, h2 * AHEAD[0] + e, 1)
                dve.wait_ge(r_ready, hh * 2 + 2)
                dve.tensor_tensor(hv, hv, ss[:, :].unsqueeze(2).broadcast_to([P, NB, DV]), ALU.mult).then_inc(hn_ready, 1)
                for g, (b0, nb) in enumerate(OUT_GROUPS):
                    dve.wait_ge(out_turned, hh * 3 + (g + 1))
                    t0, n = (b0 * P, nb * P) if b0 < NC else (SEQ, NS)
                    dve.scalar_tensor_tensor(out=gate_of(p, h2, slice(t0, t0 + n)),
                                             in0=m.bank[3 + g % 2][:, 0:n], scalar=ghcur[:, h2:h2 + 1],
                                             in1=gate_of(p, h2, slice(t0, t0 + n)), op0=ALU.mult, op1=ALU.mult).then_inc(y_ok, 1)

            for e in range(FIRST_TILES, sum(AHEAD)):
                if e == 3 * NT:
                    dve.wait_ge(spilled, 16 * KT)
                read_out(0, e)

            def pair(p, more):
                dve.wait_ge(state_out, FIRST + p * 64)
                dve.wait_ge(y_ok, FIRST + p * 6)
                dve.memset(C[:, :], 0.0).then_inc(c_ready, 1)
                dve.tensor_copy(gcur[:, :, :, :], tokg[:, :, :].rearrange("p c (g e) -> p c g e", g=3)[:, :, :, bass.ds(p * 2, 2)])
                dve.tensor_copy(dcur[0:DK, :], decb[0:DK, bass.ds(p * 2, 1), :].rearrange("p o e -> p (o e)"))
                dve.tensor_copy(dcur[DK:P, :], decb[DK:P, bass.ds(p * 2 + 1, 1), :].rearrange("p o e -> p (o e)"))
                dve.tensor_copy(ghcur[:, :], ghead[:, bass.ds(p * 2, 2)])
                step(dve.tensor_copy(selcur[:, :], m.ident[0:HA, bass.ds(p * 2, 2)]))
                for t in range(NT):
                    dve.wait_ge(w.tile_free[t], p * 6 + 6)
                dve.tensor_copy(kT[:, :], kst[:, :]).then_inc(qk_ready, 1)
                dve.tensor_copy(qT[:, :], qst[:, :]).then_inc(qk_ready, 1)
                dve.tensor_copy(qsel[:, :].rearrange("p (b t) -> p b t", t=NS + ST)[:, :, 0:ST],
                                qst[:, SEQ:T].rearrange("p (b t) -> p b t", t=ST)).then_inc(qsel_ready, 1)
                for e in range(sum(AHEAD), TILES):
                    read_out(p, e)
                dve.wait_ge(in_ready, FIRST + p * 9 + 9)
                dve.wait_ge(qk_ready, p * 2 + 2)
                dve.wait_ge(qsel_ready, p + 1)
                def u_of(h2):
                    dve.wait_ge(u_spread, FIRST + (p * 2 + h2) * 3)
                    dve.tensor_scalar(uh[0:HA, :], ub[0:HA, :], selcur[:, h2:h2 + 1], None, ALU.mult).then_inc(uh_ready, 1)

                u_of(0)
                for h2 in range(2):
                    hh = p * 2 + h2
                    for cb in range(NB + 1):
                        u = hh * NB + cb
                        if cb < NB:
                            t0, n = blocks_of(cb)
                            dve.wait_ge(d_ready, FIRST + hh * 3 + (cb // 4 + 1))
                            dve.wait_ge(s_ready, u + 1)
                            dve.wait_ge(n1_ready, FIRST + (u if cb == 0 else hh * NB + (cb - 1)))
                            dve.tensor_tensor(wt[cb % 2][0:n, 0:n], m.bank[6][0:n, 0:n], dec[0:n, t0:t0 + n], ALU.mult)\
                                .then_inc(wt_ready, 1)
                            if cb < NC:
                                if cb == 0:
                                    dve.wait_ge(dc_ready, FIRST + hh * NC)
                                dve.tensor_scalar(kw[cb % 2][:, :], ktok[:, cb, hr(h2)], dec[:, t0 + P - 1:t0 + P], None,
                                                  ALU.mult).then_inc(kw_ready, 1)
                            else:
                                dve.wait_ge(dcs_ready, FIRST + hh * 3)
                                lastcol = dec[0:NS, SEQ:T].rearrange("s (b t) -> s b t", t=ST)[:, :, ST - 1:ST]
                                dve.tensor_tensor(kws[:, :, :],
                                                  ktok[0:NS, NC, hr(h2)].unsqueeze(1).broadcast_to([NS, SB, DK]),
                                                  lastcol.broadcast_to([NS, SB, DK]), ALU.mult).then_inc(kw_ready, 1)
                        if cb >= 1:
                            pb = cb - 1
                            n = blocks_of(pb)[1]
                            if pb < NC:
                                dve.wait_ge(dc_ready, FIRST + hh * NC + (pb + 1))
                                dve.scalar_tensor_tensor(out=C[hr(h2), :], in0=C[hr(h2), :], scalar=dcur[hr(h2), pb:pb + 1],
                                                         in1=m.bank[4][hr(h2), 0:DA], op0=ALU.mult, op1=ALU.add)\
                                    .then_inc(c_ready, 1)
                            dve.wait_ge(n1_ready, FIRST + hh * NB + (pb + 1))
                            dve.wait_ge(n2_scaled, FIRST + hh * NB + (pb + 1))
                            dve.tensor_tensor(num[0:n, pb, :], m.bank[7][0:n, 0:DA], inter[0:n, :], ALU.add)\
                                .then_inc(num_ready, 1)
                        if more and cb - 1 in BEHIND[h2]:
                            read_out(p, h2 * AHEAD[0] + BEHIND[h2].index(cb - 1), 1)
                        if cb == 0:
                            dve.wait_ge(o_exp, p * 2 + (h2 + 1))
                            step(dve.tensor_scalar(gate_of(p, h2), gate_of(p, h2), 1.0, None, ALU.add))
                        elif cb <= NC:
                            part = gate_of(p, h2, slice((cb - 1) * T // NC, cb * T // NC))
                            dve.sem_inc(dve_passed, 1)
                            step(dve.reciprocal(part, part))
                    if h2 == 0:
                        u_of(1)
                    for g in range(3):
                        dve.wait_ge(dcs_ready, FIRST + hh * 3 + (g + 1))
                        for b in range(3 * g, min(3 * g + 3, SB)):
                            j = b % 3
                            last = dve.scalar_tensor_tensor(out=Cs[hr(h2), b, :], in0=Cs[hr(h2), b, :],
                                                            scalar=dcur[hr(h2), NC + b:NC + b + 1],
                                                            in1=m.bank[4][hr(h2), j * DA:(j + 1) * DA],
                                                            op0=ALU.mult, op1=ALU.add)
                        last.then_inc(cs_ready, 1)
                    dve.wait_ge(num_ready, FIRST + hh * NB + NB)
                    post(p, h2, more)

            with dve.Fori(0, HP - 1) as p:
                step.enter(p, 25)
                pair(p, True)
            step.leave(HP - 1)
            pair(HP - 1, False)


def mixer_b(nc, m, own):
    U = 24
    GROUPS = [(0, 4), (4, 4), (8, 1)]
    ZB = (3, 4, 5, 2)
    ZN = slice(2 * NS, 4 * NS)
    SLOTS, HALF = 2, NPG // 2
    TILE_AT = [0, 1, 2, 3, 4, 5, 6, 8, 17]
    TILES = len(TILE_AT)
    units = []
    for tt in range(2):
        for h2 in range(2):
            blocks = list(range(4 * tt + 3, -1, -1))
            for kb in blocks:
                units.append((h2, tt, kb, max(0, kb - 4 * tt) * P, kb == blocks[0], kb == 0))
    assert len(units) == U
    run_end = {i: r for r, i in enumerate(i for i, u in enumerate(units) if u[5])}
    TURN, Z_IN, SP_OUT, CUM, PV0 = 1, 10, 11, 12, 13
    with ExitStack() as c:
        sb = own.tensor

        qT, kT = sb("q_t", [P, T]), sb("k_t", [P, T])
        qst, kst, vst = sb("q_next", [P, T]), sb("k_next", [P, T]), sb("v_next", [P, T])
        krow, vrow = sb("k_rows", [P, NB, P]), sb("v_rows", [P, NB, P])
        zc = [sb(f"softplus{i}", [P, 512]) for i in range(2)]
        sp = [sb(f"sp{i}", [P, 512]) for i in range(2)]
        later = [sb(f"sp_later{i}", [P, 512]) for i in range(2)]
        a = [sb(f"weights{i}", [P, 512]) for i in range(2)]
        pages = [sb(f"pages{i}", [P, HALF, P]) for i in range(2 * SLOTS)]
        kpT = [sb(f"page_keys_t{i}", [P, NPG * PAGE]) for i in range(2)]
        zcs, sps, laters, as_ = m.sq[0][:, 0:512], m.sq[1][:, 0:512], m.acc[:, 0:512], m.sq[0][:, 512:1024]
        zcn, spn, an = sb("softplus_new", [NS, 2 * NS]), sb("sp_new", [NS, 2 * NS]), sb("weights_new", [NS, 2 * NS])
        qd = sb("q_sample", [P, SB, 2, ST])
        bias, bcur = sb("bias", [P, HB]), sb("bias_now", [P, 2])

        w, s = weight_sems(own.sem), norm_sems(own.sem)
        landed, spilled, filled, chain = own.sem("b_landed"), own.sem("h_spilled"), own.sem("fills"), own.sem("dve_step")
        in_turned, in_ready = own.sem("rows_turned"), own.sem("rows_ready")
        stored = own.sem("rows_stored")
        z_ready, zc_ready, e_ready, ln_ready = own.sem("z_ready"), own.sem("z_clamped"), own.sem("exp_ready"), own.sem("ln_ready")
        sp_ready, later_ready = own.sem("sp_ready"), own.sem("sp_later_ready")
        cum_ready, a_ready, pv_ready, y_ok = own.sem("sums_ready"), own.sem("weights_ready"), own.sem("pv_ready"), own.sem("y_tile")
        page_in, v_used = [own.sem(f"pages_in{i}") for i in range(2 * SLOTS)], own.sem("value_pages_used")
        k_turned, kt_act, kt_dve, zs_done = own.sem("keys_turned"), own.sem("keys_t_low"), own.sem("keys_t_high"), own.sem("zs_by_seq")
        pvs_done = own.sem("pvs_by_seq")
        qd_ready, zs_ready, zcs_ready, es_ready = own.sem("q_sample_ready"), own.sem("zs_ready"), own.sem("zs_clamped"), own.sem("es_ready")
        lns_ready, sps_ready, cums_ready, as_ready = own.sem("lns_ready"), own.sem("sps_ready"), own.sem("sums_s_ready"), own.sem("weights_s_ready")
        ys_ok = own.sem("ys_tile")
        qk_ready = own.sem("q_and_k_taken")
        pe_passed, sp_passed = own.sem("pe_passed"), own.sem("sp_passed")

        wq_v = m.d["w_q_b"][0].rearrange("(k p) (m j) -> m p k j", p=P, j=P)
        wkv_v = m.d["w_kv"].rearrange("(k p) (m j) -> m p k j", p=P, j=P)
        panels = []
        for pp in range(2):
            panels += [(lambda i, pp=pp: wq_v[i * 2 + pp], NT, m.g_mix[1]),
                       (lambda i, pp=pp: wkv_v[i * 2 + pp], NT, m.g_kv),
                       (lambda i, pp=pp: wkv_v[i * 2 + (pp + 8)], NT, m.g_kv)]
        kp_d, vp_d = (x[0].rearrange("(c p) (q h) e -> q p c (h e)", p=P, h=2) for x in (m.d["k_prompt"], m.d["v_prompt"]))
        ks_d, vs_d = (x.rearrange("b t (q h) e -> q (b t) (h e)", h=2) for x in (m.d["k_sample"], m.d["v_sample"]))
        ck_d, cv_d = (x.rearrange("(b g) s (q h) e -> q b s g (h e)", b=2 * SB, h=2) for x in (m.k_pages, m.v_pages))
        block = c.enter_context(nc.Block())

        PAGES_IN = 2 * SB // SLOTS * 16

        def hr(h2):
            return slice(h2 * DH, (h2 + 1) * DH)

        def by_page(ap):
            return ap.rearrange("p (x g t) -> p x g t", g=NPG, t=ST)

        @block.sync
        def _(eng):
            for count in (stored,):
                eng.sem_inc(count, FIRST)
            eng.dma_start(bias[:, :], m.d["sb_bias"][0:1, :].broadcast_to([P, HB]))\
                .then_inc(landed, 16)

            def weights(i, j):
                n = i * 6 + j
                if not isinstance(n, int) or n >= 2:
                    eng.wait_ge(w.split, n - 1)
                ap = panels[j % 6][0](i if j < 6 else i + 1)
                eng.dma_start(m.wraw[j % 2][:, :].rearrange("p (k j) -> p k j", j=P), ap).then_inc(w.loaded[j % 2], 16)

            for j in range(3):
                weights(0, j)
            for k in range(KT):
                eng.dma_start(m.spill[k], m.h[:, k, :]).then_inc(spilled, 16)

            def load_pages(pair, y, r, src):
                eng.dma_start(pages[y][:, :, :], src[pair, r * (2 * SLOTS) + y]).then_inc(page_in[y], 16)

            def pair_loads(i, pp, more):
                pair = i * 2 + pp
                for y in range(2 * SLOTS):
                    eng.wait_ge(v_used, pair * (2 * SB) + (2 * (SB - SLOTS) + y + 1))
                    load_pages(pair, y, 0, ck_d)
                if more:
                    for j in range(3):
                        weights(i, 3 * pp + 3 + j)
                with eng.Fori(1, SB // SLOTS) as r:
                    for y in range(2 * SLOTS):
                        eng.wait_ge(k_turned, pair * (2 * SB) + r * (2 * SLOTS) + (y + 1 - 2 * SLOTS))
                        load_pages(pair, y, r, ck_d)
                eng.wait_ge(in_ready, FIRST + pair * 6 + 6)
                eng.sem_inc(sp_passed, 1)
                eng.dma_start(kp_d[pair], krow[:, 0:NC, :]).then_inc(stored, 16)
                eng.dma_start(vp_d[pair], vrow[:, 0:NC, :]).then_inc(stored, 16)
                eng.dma_start(ks_d[pair], krow[0:NS, NC, :]).then_inc(stored, 16)
                eng.dma_start(vs_d[pair], vrow[0:NS, NC, :]).then_inc(stored, 16)
                for y in range(2 * SLOTS):
                    eng.wait_ge(k_turned, pair * (2 * SB) + (2 * (SB - SLOTS) + y + 1))
                    load_pages(pair, y, 0, cv_d)
                with eng.Fori(1, SB // SLOTS) as r:
                    for y in range(2 * SLOTS):
                        eng.wait_ge(v_used, pair * (2 * SB) + r * (2 * SLOTS) + (2 * SB + y + 1 - 2 * SLOTS))
                        load_pages(pair, y, r, cv_d)

            with eng.Fori(0, HB // 4 - 1) as i:
                for pp in range(2):
                    pair_loads(i, pp, True)
            pair_loads(HB // 4 - 1, 0, True)
            pair_loads(HB // 4 - 1, 1, False)
            eng.wait_ge(stored, FIRST + 64 * (HB // 2))
            eng.wait_ge(spilled, 16 * KT)

        @block.gpsimd
        def _(pool):
            pool.memset(qd[:, :, :, :], 0.0).then_inc(filled, 1)
            weight_splits(pool, m, w, [(HB // 4, panels)])

        @block.tensor
        def _(pe):
            for count in (cum_ready,):
                pe.sem_inc(count, FIRST)
            def turn_in(pair, g0, tile):
                for g, (b0, nb) in enumerate(GROUPS):
                    g += g0
                    pe.wait_ge(in_ready, FIRST + pair * 6 + max(g - 1, 0))
                    for j in range(nb):
                        t0, n = blocks_of(b0 + j)
                        last = pe.transpose(m.bank[3 + g % 2][0:n, j * P:(j + 1) * P], tile[:, t0:t0 + n], m.ident[:, :])
                    last.then_inc(in_turned, 1)

            def z(pair, i):
                h2, tt, kb, off, _, _ = units[i]
                if i >= 4:
                    pe.wait_ge(a_ready, FIRST + pair * U + (i - 3))
                q0 = tt * 512 + off
                pe.matmul(m.bank[ZB[i % 4]][:, 0:512 - off], kT[hr(h2), kb * P:(kb + 1) * P],
                          qT[hr(h2), q0:tt * 512 + 512], start=True, stop=True).then_inc(z_ready, 1)

            def sums(pair, i):
                h2, tt, kb, off, first, _ = units[i]
                n, bank = 512 - off, m.bank[ZB[i % 4]]
                pe.wait_ge(sp_ready, pair * U + (i + 1))
                last = pe.matmul(bank[:, 0:n], m.negtri[:, :], sp[i % 2][:, 0:n], start=False, stop=True,
                                 skip_group_check=True)
                diagonal = kb >= 4 * tt
                if not first:
                    pe.wait_ge(later_ready, pair * U + i)
                    skip = P if diagonal else 0
                    last = pe.matmul(bank[:, skip:n], m.negones[:, :], later[(i - 1) % 2][:, off + skip:512], start=False,
                                     stop=True, skip_group_check=True)
                if diagonal:
                    last = pe.matmul(bank[:, 0:P], m.identb[:, :], m.strict[:, :], start=False, stop=True,
                                     skip_group_check=True)
                last.then_inc(cum_ready, 1)

            def pv(pair, i):
                h2, tt, kb, off, first, last = units[i]
                pe.wait_ge(a_ready, FIRST + pair * U + (i + 1))
                if first:
                    pe.wait_ge(y_ok, FIRST + pair * 4 + (0 if tt == 0 else 1 + h2))
                pe.matmul(m.bank[6][hr(h2), off:512], vrow[:, kb, hr(h2)], a[i % 2][:, 0:512 - off], start=first, stop=last,
                          skip_group_check=True).then_inc(pv_ready, 1)

            def turn_pages(pair, b, half):
                y = 2 * (b % SLOTS) + half
                if b == 0 and half == 0:
                    pe.wait_ge(ys_ok, FIRST + pair * 2)
                pe.wait_ge(page_in[y], pair * PAGES_IN + (b // SLOTS + 1) * 16)
                pe.wait_ge(kt_act if half else kt_dve, FIRST + pair * SB + (b + half))
                for g in range(HALF):
                    last = pe.transpose(m.bank[0][:, g * P:(g + 1) * P], pages[y][:, g, :], m.ident[:, :])
                last.then_inc(k_turned, 1)

            def z_pages(pair, b):
                pe.wait_ge(kt_act, FIRST + pair * SB + (b + 1))
                pe.wait_ge(kt_dve, FIRST + pair * SB + (b + 1))
                if b == 0:
                    pe.wait_ge(qd_ready, pair * 2 + 2)
                    pe.wait_ge(as_ready, FIRST + pair * 4)
                for g in range(NPG):
                    out = m.bank[7][:, :].rearrange("p (h x) -> p h x", h=2)[:, :, b * 32 + g * ST:b * 32 + g * ST + ST]
                    last = pe.matmul(out, kpT[b % 2][:, g * PAGE:(g + 1) * PAGE], qd[:, b, :, :], start=(b == 0 and g == 0),
                                     stop=True, skip_group_check=True)
                last.then_inc(zs_done, 1)

            def z_new(pair):
                pe.matmul(m.bank[0][0:NS, ZN].rearrange("p (h b t) -> p h b t", h=2, t=ST), kT[:, SEQ:T], qd[:, :, :, :].rearrange("p b h t -> p h b t"),
                          start=True, stop=True).then_inc(zs_ready, 1)

            def sums_s(pair):
                pe.wait_ge(sps_ready, pair * 2 + 2)
                pe.matmul(m.bank[7][:, :], m.negtri[:, :], sps, start=False, stop=True, skip_group_check=True)
                pe.matmul(by_page(m.bank[7][:, :])[:, :, 0:NPG - 1, :], m.negones[:, :],
                          by_page(laters)[:, :, 0:NPG - 1, :], start=False, stop=True, skip_group_check=True)
                pe.matmul(by_page(m.bank[7][:, :]), m.negones[0:NS, :],
                          spn[:, :].rearrange("s (x t) -> s x t", t=ST).unsqueeze(2).broadcast_to([NS, 2 * SB, NPG, ST]),
                          start=False, stop=True, skip_group_check=True).then_inc(cums_ready, 1)
                pe.matmul(m.bank[0][0:NS, ZN], m.negtri[0:NS, 0:NS], spn[:, :], start=False, stop=True, skip_group_check=True)
                pe.matmul(m.bank[0][0:NS, ZN], m.identb[0:NS, 0:NS], m.new_mask[:, :], start=False, stop=True,
                          skip_group_check=True).then_inc(cums_ready, 1)

            def pv_pages(pair, b):
                if b == 0:
                    pe.wait_ge(as_ready, FIRST + pair * 4 + 4)
                    pe.wait_ge(kt_act, FIRST + pair * SB + SB)
                heads = as_[:, :].rearrange("p (h x) -> p h x", h=2)
                for half in range(2):
                    y = 2 * (b % SLOTS) + half
                    pe.wait_ge(page_in[y], pair * PAGES_IN + ((SB + b) // SLOTS + 1) * 16)
                    for g in range(HALF):
                        c0 = b * 32 + (half * HALF + g) * ST
                        last = pe.matmul(m.bank[0][:, b * 8:b * 8 + 8].rearrange("p (h t) -> p h t", h=2),
                                         pages[y][:, g, :], heads[:, :, c0:c0 + ST],
                                         start=(b == 0 and half == 0 and g == 0), stop=False, skip_group_check=True)
                    last.then_inc(v_used, 1)
                pe.matmul(m.bank[0][:, b * 8:b * 8 + 8].rearrange("p (h t) -> p h t", h=2), vrow[0:NS, NC, :],
                          an[:, :].rearrange("s (h b t) -> s h b t", h=2, b=SB)[:, :, b, :], start=False, stop=True,
                          skip_group_check=True).then_inc(pvs_done, 1)

            pe.sem_inc(pvs_done, SB)

            def tile_of(i2, n, e):
                j, t = e // NT, e % NT
                pe.wait_ge(w.split, i2 * 6 + (n + j + 1))
                pe.wait_ge(w.tile_free[0], i2 * (2 * TILES) + (n * NT + e + 1))
                dense_tile(pe, m.whi[(n + j) % 2], m.wlo[(n + j) % 2], KT, 0, m.xhi, m.xlo, t, m.bank[1])\
                    .then_inc(w.tile_ready, 1)

            def attend(i2, pp, more):
                pair = i2 * 2 + pp
                pe.wait_ge(w.tile_free[0], pair * TILES + (TILES + 1))
                turn_in(pair, 0, kst)
                turn_in(pair, 3, vst)
                pe.wait_ge(in_ready, FIRST + pair * 6 + 6)
                pe.wait_ge(qk_ready, pair * 2 + 2)
                z(pair, 0)
                z(pair, 1)
                z(pair, 2)
                for i in range(U):
                    if i >= 1:
                        pv(pair, i - 1)
                    if TURN <= i < TURN + SB:
                        turn_pages(pair, i - TURN, 0)
                    sums(pair, i)
                    if i + 3 < U:
                        z(pair, i + 3)
                    if more and i in TILE_AT:
                        tile_of(i2, 3 * pp + 3, TILE_AT.index(i))
                    if TURN <= i < TURN + SB:
                        turn_pages(pair, i - TURN, 1)
                    if TURN + 1 <= i < TURN + 1 + SB:
                        z_pages(pair, i - TURN - 1)
                    if i == TURN + SB:
                        z_new(pair)
                    if i == CUM:
                        sums_s(pair)
                    if PV0 <= i < PV0 + SB:
                        pv_pages(pair, i - PV0)
                pv(pair, U - 1)

            pe.sem_inc(w.tile_free[0], 1)
            pe.sem_inc(v_used, 2 * SB)
            dense_first(pe, m, w, 0, 0, 0, s.x)
            norm_pe(pe, m, s)
            for e in range(NT, TILES):
                pe.wait_ge(w.split, e // NT + 1)
                pe.wait_ge(w.tile_free[0], e - NT + 2)
                slot = (e // NT) % 2
                dense_tile(pe, m.whi[slot], m.wlo[slot], KT, 0, m.xhi, m.xlo, e % NT, m.bank[e % NT])\
                    .then_inc(w.tile_ready, 1)
            with pe.Fori(0, HB // 4 - 1) as i2:
                attend(i2, 0, True)
                attend(i2, 1, True)
            attend(HB // 4 - 1, 0, True)
            attend(HB // 4 - 1, 1, False)

        @block.scalar
        def _(act):
            for count in (a_ready, in_ready, as_ready, kt_act):
                act.sem_inc(count, FIRST)
            norm_act(act, m, s, m.h, None)
            norm_act_rs(act, m, s)

            def rows(pair, g0, dst):
                for g, (b0, nb) in enumerate(GROUPS):
                    n = P if g < 2 else NS
                    act.wait_ge(in_turned, pair * 6 + (g + g0 + 1))
                    src = m.bank[3 + (g + g0) % 2][0:n, :].rearrange("p (j e) -> p j e", e=P)[:, 0:nb, :]
                    act.copy(dst[0:n, b0:b0 + nb, :], src).then_inc(in_ready, 1)

            def softplus(pair, i):
                n = 512 - units[i][3]
                act.wait_ge(zc_ready, pair * U + (i + 1))
                act.activation(zc[i % 2][:, 0:n], zc[i % 2][:, 0:n], ACT.Exp).then_inc(e_ready, 1)
                act.wait_ge(e_ready, pair * U + (i + 1))
                act.activation(zc[i % 2][:, 0:n], zc[i % 2][:, 0:n], ACT.Ln, bias=1.0).then_inc(ln_ready, 1)

            def weights(pair, i):
                h2, n = units[i][0], 512 - units[i][3]
                act.wait_ge(cum_ready, FIRST + pair * U + (i + 1))
                if i >= 2:
                    act.wait_ge(pv_ready, pair * U + (i - 1))
                act.activation(a[i % 2][:, 0:n], m.bank[ZB[i % 4]][:, 0:n], ACT.Exp, bias=bcur[:, h2:h2 + 1])\
                    .then_inc(a_ready, 1)

            with act.Fori(0, HB // 4) as i2:
                for pp in range(2):
                    pair = i2 * 2 + pp
                    act.wait_ge(stored, FIRST + pair * 64)
                    rows(pair, 0, krow)
                    rows(pair, 3, vrow)
                    softplus(pair, 0)
                    for i in range(U):
                        if i + 1 < U:
                            softplus(pair, i + 1)
                        weights(pair, i)
                        if TURN <= i < TURN + SB:
                            b = i - TURN
                            act.wait_ge(k_turned, pair * 16 + (2 * b + 1))
                            if b >= 2:
                                act.wait_ge(zs_done, pair * SB + (b - 1))
                            act.copy(kpT[b % 2][:, 0:512], m.bank[0][:, :]).then_inc(kt_act, 1)
                        if i == Z_IN:
                            for j, tile in enumerate((zcs, zcn[:, :])):
                                act.wait_ge(zcs_ready, pair * 4 + (2 * j + 2))
                                act.activation(tile, tile, ACT.Exp).then_inc(es_ready, 1)
                                act.wait_ge(es_ready, pair * 2 + (j + 1))
                                act.activation(tile, tile, ACT.Ln, bias=1.0).then_inc(lns_ready, 1)
                        if i == CUM:
                            for h2 in range(2):
                                if h2 == 0:
                                    act.wait_ge(cums_ready, pair * 2 + 2)
                                half, nh, zh = slice(256 * h2, 256 * h2 + 256), slice(NS * h2, NS * h2 + NS), slice(NS * (2 + h2), NS * (3 + h2))
                                act.activation(as_[:, half], m.bank[7][:, half], ACT.Exp, bias=bcur[:, h2:h2 + 1])\
                                    .then_inc(as_ready, 1)
                                act.activation(an[:, nh], m.bank[0][0:NS, zh], ACT.Exp, bias=bcur[0:NS, h2:h2 + 1])\
                                    .then_inc(as_ready, 1)

        @block.vector
        def _(dve):
            for count in (kt_dve, y_ok, ys_ok):
                dve.sem_inc(count, FIRST)
            norm_dve(dve, m, s, m.h, None)
            step = Pipe(dve, chain)
            dve.wait_ge(landed, 16)
            dve.wait_ge(filled, 1)
            dve.wait_ge(spilled, 16 * KT)
            dve.wait_ge(s.rs, 1)

            def read_out(i2, n, e, bank=1):
                j, t = e // NT, e % NT
                ts = slice(t * TW, (t + 1) * TW)
                dve.wait_ge(w.tile_ready, i2 * (2 * TILES) + (n * NT + e + 1))
                if j == 0:
                    ins = dve.scalar_tensor_tensor(out=qst[:, ts], in0=m.bank[bank][:, 0:TW], scalar=DH ** -0.5,
                                                   in1=m.rs[:, ts], op0=ALU.mult, op1=ALU.mult)
                else:
                    ins = dve.tensor_tensor((kst if j == 1 else vst)[:, ts], m.bank[bank][:, 0:TW], m.rs[:, ts], ALU.mult)
                ins.then_inc(w.tile_free[0], 1)

            def clamp(pair, i):
                h2, n = units[i][0], 512 - units[i][3]
                dve.wait_ge(z_ready, pair * U + (i + 1))
                if i >= 2:
                    dve.wait_ge(sp_ready, pair * U + (i - 1))
                dve.tensor_scalar(zc[i % 2][:, 0:n], m.bank[ZB[i % 4]][:, 0:n], bcur[:, h2:h2 + 1], CLAMP, ALU.add, ALU.min)\
                    .then_inc(zc_ready, 1)

            def softplus(pair, i):
                h2, tt, kb, off, first, last = units[i]
                n = 512 - off
                dve.wait_ge(ln_ready, pair * U + (i + 1))
                if i >= 2:
                    dve.wait_ge(cum_ready, FIRST + pair * U + (i - 1))
                args = dict(out=sp[i % 2][:, 0:n], in0=m.bank[ZB[i % 4]][:, 0:n], scalar=bcur[:, h2:h2 + 1],
                            in1=zc[i % 2][:, 0:n], op0=ALU.add, op1=ALU.max)
                if kb >= 4 * tt:
                    step(dve.scalar_tensor_tensor(**args))
                    dve.tensor_tensor(sp[i % 2][:, 0:P], sp[i % 2][:, 0:P], m.strict01[:, :], ALU.mult).then_inc(sp_ready, 1)
                else:
                    dve.scalar_tensor_tensor(**args).then_inc(sp_ready, 1)
                dve.wait_ge(sp_ready, pair * U + (i + 1))
                if i:
                    dve.wait_ge(cum_ready, FIRST + pair * U + i)
                    dve.wait_ge(later_ready, pair * U + i)
                new, old = later[i % 2], later[(i - 1) % 2]
                if first:
                    dve.tensor_copy(new[:, off:512], sp[i % 2][:, 0:n]).then_inc(later_ready, 1)
                    return
                skip = P if kb >= 4 * tt else 0
                if skip:
                    dve.tensor_copy(new[:, off:off + P], sp[i % 2][:, 0:P])
                dve.tensor_tensor(new[:, off + skip:512], old[:, off + skip:512], sp[i % 2][:, skip:n], ALU.add)\
                    .then_inc(later_ready, 1)

            def run_out(pair, r):
                h2, tt = r % 2, r // 2
                last = [i for i, q in run_end.items() if q == r][0]
                dve.wait_ge(pv_ready, pair * U + (last + 1))
                dve.tensor_copy(m.h[hr(h2), bass.ds(pair, 1), tt * 512:tt * 512 + 512].rearrange("p o t -> p (o t)"),
                                m.bank[6][hr(h2), :]).then_inc(y_ok, 1)

            def attend(i2, pp, more):
                pair = i2 * 2 + pp
                dve.wait_ge(a_ready, FIRST + pair * U)
                step(dve.tensor_copy(bcur[:, :], bias[:, bass.ds(pair * 2, 2)]))
                dve.wait_ge(w.tile_free[0], pair * TILES + (TILES + 1))
                dve.wait_ge(pvs_done, pair * SB + SB)
                dve.wait_ge(cum_ready, FIRST + pair * U)
                dve.tensor_copy(kT[:, :], kst[:, :]).then_inc(qk_ready, 1)
                dve.tensor_copy(qT[:, :], qst[:, :]).then_inc(qk_ready, 1)
                for h2 in range(2):
                    dve.tensor_copy(qd[hr(h2), :, h2, :], qst[hr(h2), SEQ:T].rearrange("p (b t) -> p b t", t=ST))\
                        .then_inc(qd_ready, 1)
                clamp(pair, 0)
                clamp(pair, 1)
                for i in range(U):
                    softplus(pair, i)
                    if i + 2 < U:
                        clamp(pair, i + 2)
                    if i - 2 in run_end:
                        run_out(pair, run_end[i - 2])
                    if more and i - 1 in TILE_AT:
                        if i - 1 == TILE_AT[0]:
                            dve.wait_ge(qk_ready, pair * 2 + 2)
                            dve.wait_ge(qd_ready, pair * 2 + 2)
                            dve.wait_ge(in_turned, pair * 6 + 6)
                        read_out(i2, 3 * pp + 3, TILE_AT.index(i - 1))
                    if TURN <= i < TURN + SB:
                        b = i - TURN
                        dve.wait_ge(k_turned, pair * 16 + (2 * b + 2))
                        if b >= 2:
                            dve.wait_ge(zs_done, pair * SB + (b - 1))
                        dve.tensor_copy(kpT[b % 2][:, 512:1024], m.bank[0][:, :]).then_inc(kt_dve, 1)
                    if i == Z_IN:
                        dve.wait_ge(zs_done, pair * SB + SB)
                        for h2 in range(2):
                            half = slice(256 * h2, 256 * h2 + 256)
                            dve.tensor_scalar(zcs[:, half], m.bank[7][:, half], bcur[:, h2:h2 + 1], CLAMP, ALU.add,
                                              ALU.min).then_inc(zcs_ready, 1)
                        dve.wait_ge(zs_ready, pair + 1)
                        for h2 in range(2):
                            nh, zh = slice(NS * h2, NS * h2 + NS), slice(NS * (2 + h2), NS * (3 + h2))
                            dve.tensor_scalar(zcn[:, nh], m.bank[0][0:NS, zh], bcur[0:NS, h2:h2 + 1], CLAMP, ALU.add,
                                              ALU.min).then_inc(zcs_ready, 1)
                    if i == SP_OUT:
                        dve.wait_ge(lns_ready, pair * 2 + 2)
                        for h2 in range(2):
                            half, nh, zh = slice(256 * h2, 256 * h2 + 256), slice(NS * h2, NS * h2 + NS), slice(NS * (2 + h2), NS * (3 + h2))
                            dve.scalar_tensor_tensor(out=spn[:, nh], in0=m.bank[0][0:NS, zh], scalar=bcur[0:NS, h2:h2 + 1],
                                                     in1=zcn[:, nh], op0=ALU.add, op1=ALU.max)
                            step(dve.scalar_tensor_tensor(out=sps[:, half], in0=m.bank[7][:, half],
                                                          scalar=bcur[:, h2:h2 + 1], in1=zcs[:, half], op0=ALU.add,
                                                          op1=ALU.max))
                        dve.tensor_tensor(spn[:, :], spn[:, :], m.new01[:, :], ALU.mult).then_inc(sps_ready, 1)
                        lp, spp = by_page(laters), by_page(sps)
                        step(dve.tensor_copy(lp[:, :, NPG - 2, :], spp[:, :, NPG - 1, :]))
                        for g in range(NPG - 3, -1, -1):
                            ins = dve.tensor_tensor(lp[:, :, g, :], lp[:, :, g + 1, :], spp[:, :, g + 1, :], ALU.add)
                            if g:
                                step(ins)
                        ins.then_inc(sps_ready, 1)
                    if i == PV0 + SB:
                        dve.wait_ge(pvs_done, pair * SB + 2 * SB)
                        for h2 in range(2):
                            ysv = m.h[hr(h2), bass.ds(pair, 1), SEQ:T].rearrange("p o (b t) -> p (o b) t", t=ST)
                            bv = m.bank[0][hr(h2), 0:64].rearrange("p (b h t) -> p b h t", h=2, t=ST)[:, :, h2, :]
                            dve.tensor_copy(ysv, bv).then_inc(ys_ok, 1)
                run_out(pair, 3)

            for e in range(TILES):
                read_out(0, 0, e, e % NT)
            with dve.Fori(0, HB // 4 - 1) as i2:
                step.enter(i2, 2 * (1 + 16 + 2 + 1 + NPG - 3))
                attend(i2, 0, True)
                attend(i2, 1, True)
            step.leave(HB // 4 - 1)
            attend(HB // 4 - 1, 0, True)
            attend(HB // 4 - 1, 1, False)


def out_and_mlp(nc, m, own, w_out, w_up, w_down, gain, gather):
    with ExitStack() as c:
        UT = 4
        CH = DFF // (UT * P)
        uhi = own.tensor("u_hi", [P, UT, T], F32R)
        ulo = own.tensor("u_lo", [P, UT, T], F32R)
        relu = [own.tensor(f"relu{t}", [P, TW], F32) for t in range(NT)]
        sqr = [own.tensor(f"relu_sq{t}", [P, TW], F32) for t in range(NT)]
        w, s = weight_sems(own.sem), norm_sems(own.sem)
        y_hi, y_x = own.sem("y_hi_ready"), own.sem("y_split")
        gathered = own.sem("pages_gathered")
        h_back = [own.sem(f"h_back{k}") for k in range(KT)]
        scaled, sq_ready, hi_ready, u_ready = own.sem("relu_scaled"), own.sem("relu_sq_ready"), own.sem("u_hi_ready"), own.sem("u_ready")
        out_v = w_out.rearrange("(k p) (m j) -> m p k j", p=P, j=P)
        up_v = w_up.rearrange("(k p) (c u j) -> u c p k j", p=P, j=P, u=UT)
        down_v = w_down.rearrange("(c k p) (q j) -> q c p k j", k=UT, p=P, j=2 * P)
        QD = D // (2 * P)
        stages = [(KT // 2, [(lambda i, s_=s_: out_v[i * 2 + s_], NT) for s_ in range(2)]),
                  (CH, [(lambda i, u=u: up_v[u, i], NT) for u in range(UT)]
                   + [(lambda i, q=q: down_v[q, i], 2 * NT) for q in range(QD)])]
        TILES_OUT, TILES_C = KT * NT, UT * NT + QD * 2 * NT
        USES_OUT, USES_C = KT, UT + QD * 2
        block = c.enter_context(nc.Block())

        @block.sync
        def _(sp):
            def behind(i, j):
                gather_page(nc, sp, m, i * (UT + QD) + j, m.d["cache_v"], m.v_pages, gathered)
            weight_loads(sp, m, w, stages, behind if gather else None)
            if gather:
                sp.wait_ge(gathered, 16 * SB * NPG)

        @block.gpsimd
        def _(pool):
            weight_splits(pool, m, w, stages)

        @block.tensor
        def _(pe):
            dense_first(pe, m, w, 0, 0, 0, y_x)
            for n in range(1, KT):
                dense_panel(pe, m, w, n, n % 2, n)
            norm_pe(pe, m, s)
            dense_first(pe, m, w, KT, 0, USES_OUT, s.x)

            def turn(i, first):
                for u in range(first, UT):
                    dense_panel(pe, m, w, i * (UT + QD) + (KT + u), u % 2, i * USES_C + (USES_OUT + u))
                for q in range(QD):
                    pe.wait_ge(w.split, i * (UT + QD) + (KT + UT + q + 1))
                    for mm in range(2):
                        for t in range(NT):
                            pe.wait_ge(w.tile_free[t], i * USES_C + (USES_OUT + UT + 2 * q + mm))
                            if q == 0 and mm == 0:
                                pe.wait_ge(u_ready, i * (UT * NT) + ((UT - 1) * NT + t + 1))
                            dense_tile(pe, m.whi[q % 2], m.wlo[q % 2], UT, mm * P, uhi, ulo, t, m.bank[t])\
                                .then_inc(w.tile_ready, 1)
            turn(0, 1)
            with pe.Fori(1, CH) as i:
                turn(i, 0)

        @block.scalar
        def _(act):
            for k in range(KT):
                act.activation(m.xhi[:, k, :], m.h[:, k, :], ACT.Copy).then_inc(y_hi, 1)
            for k in range(KT):
                act.wait_ge(y_x, k + 1)
                act.dma_start(m.h[:, k, :], m.spill[k]).then_inc(h_back[k], 16)
            for k in range(KT):
                for t in range(NT):
                    act.wait_ge(w.tile_free[t], k + 1)
                norm_square(act, m, s, m.h, k)
            act.wait_ge(w.tile_ready, TILES_OUT)
            norm_act_hi(act, m, s, m.h, gain)
            norm_act_rs(act, m, s)
            with act.Fori(0, CH) as i:
                for u in range(UT):
                    for t in range(NT):
                        n = u * NT + t
                        act.wait_ge(w.tile_ready, i * TILES_C + (TILES_OUT + n + 1))
                        act.activation(relu[t][:, :], m.bank[t][:, 0:TW], ACT.Relu).then_inc(w.tile_free[t], 1)
                        act.wait_ge(scaled, i * (UT * NT) + (n + 1))
                        act.activation(sqr[t][:, :], relu[t][:, :], ACT.Square).then_inc(sq_ready, 1)

        @block.vector
        def _(dve):
            for k in range(KT):
                dve.wait_ge(y_hi, k + 1)
                dve.tensor_tensor(m.xlo[:, k, :], m.h[:, k, :], f32(m.xhi[:, k, :]), ALU.subtract).then_inc(y_x, 1)
            for k in range(KT):
                dve.wait_ge(h_back[k], 16)
                for t in range(NT):
                    dve.wait_ge(w.tile_ready, k * NT + t + 1)
                    ht = m.h[:, k, t * TW:(t + 1) * TW]
                    dve.tensor_tensor(ht, m.bank[t][:, 0:TW], ht, ALU.add).then_inc(w.tile_free[t], 1)
                if k:
                    norm_add(dve, m, s, k - 1)
            norm_add(dve, m, s, KT - 1)
            for t in range(NT):
                dve.wait_ge(w.tile_free[t], USES_OUT)
            norm_dve_lo(dve, m, s, m.h, gain)
            dve.wait_ge(s.rs, 1)
            with dve.Fori(0, CH) as i:
                for u in range(UT):
                    for t in range(NT):
                        n, toks = u * NT + t, slice(t * TW, (t + 1) * TW)
                        dve.wait_ge(w.tile_free[t], i * USES_C + (USES_OUT + u + 1))
                        dve.tensor_tensor(relu[t][:, :], relu[t][:, :], m.rs[:, toks], ALU.mult).then_inc(scaled, 1)
                        dve.wait_ge(sq_ready, i * (UT * NT) + (n + 1))
                        dve.tensor_copy(uhi[:, u, toks], sqr[t][:, :]).then_inc(hi_ready, 1)
                        dve.wait_ge(hi_ready, i * (UT * NT) + (n + 1))
                        dve.tensor_tensor(ulo[:, u, toks], sqr[t][:, :], f32(uhi[:, u, toks]), ALU.subtract)\
                            .then_inc(u_ready, 1)
                for q in range(QD):
                    for mm in range(2):
                        for t in range(NT):
                            dve.wait_ge(w.tile_ready,
                                        i * TILES_C + (TILES_OUT + UT * NT + (2 * q + mm) * NT + t + 1))
                            ht = m.h[:, 2 * q + mm, t * TW:(t + 1) * TW]
                            dve.tensor_tensor(ht, m.bank[t][:, 0:TW], ht, ALU.add).then_inc(w.tile_free[t], 1)


INPUTS = ["x_prompt", "x_sample", "state_c", "state_n", "state_m", "cache_k", "cache_v", "page_table", "norm_mix",
          "norm_mlp", "w_in_a", "b_i", "b_f", "head_norm_a", "w_out_a", "norm_kv", "w_kv", "w_q_b", "w_out_b",
          "sb_bias", "w_up", "w_down", "norm_final"]
OUTPUTS = [("y_prompt", (1, SEQ, D)), ("y_sample", (SB, ST, D)),
           ("c_prompt", (1, 1, HA, DK, DV)), ("n_prompt", (1, 1, HA, DK)), ("m_prompt", (1, 1, HA)),
           ("k_prompt", (1, SEQ, HB, DH)), ("v_prompt", (1, SEQ, HB, DH)),
           ("c_sample", (1, SB, HA, DK, DV)), ("n_sample", (1, SB, HA, DK)), ("m_sample", (1, SB, HA)),
           ("k_sample", (SB, ST, HB, DH)), ("v_sample", (SB, ST, HB, DH))]


def program(nc, d):
    with ExitStack() as c:
        def sb(name, shape, dt=F32):
            return c.enter_context(nc.sbuf_tensor(name, shape, dt))

        m = Fields()
        m.d = d
        m.h = sb("h", [P, KT, T])
        m.xhi, m.xlo = sb("x_hi", [P, KT, T], F32R), sb("x_lo", [P, KT, T], F32R)
        m.wraw = [sb(f"w_raw{i}", [P, D]) for i in range(2)]
        m.whi = [sb(f"w_hi{i}", [P, D], F32R) for i in range(2)]
        m.wlo = [sb(f"w_lo{i}", [P, D], F32R) for i in range(2)]
        m.rs, m.acc = sb("rms_inverse", [P, T]), sb("squares", [P, T])
        m.sq = [sb(f"square{i}", [P, T]) for i in range(2)]
        m.ident, m.identb = sb("identity", [P, P]), sb("identity_bf16", [P, P], BF16)
        m.ones, m.negones, m.negtri = sb("ones", [P, P]), sb("minus_ones", [P, P]), sb("minus_later", [P, P])
        m.causal, m.strict, m.strict01 = sb("causal", [P, P], BF16), sb("strict", [P, P], BF16), sb("strict01", [P, P])
        m.causal_s = sb("causal_sample", [NS, NS], BF16)
        m.new_mask, m.new01 = sb("new_mask", [NS, 2 * NS], BF16), sb("new01", [NS, 2 * NS])
        m.eps = sb("eps", [P, 1])
        m.ptab = sb("page_numbers", [1, SB * NPG], I32)
        m.k_pages, m.v_pages = (nc.dram_tensor(name, [SB * NPG, PAGE, HB, DH], F32, kind="Internal").ap()
                                for name in ("k_pages", "v_pages"))
        m.g_mix = [sb(f"g_mix{l}", [P, KT]) for l in range(2)]
        m.g_mlp = [sb(f"g_mlp{l}", [P, KT]) for l in range(2)]
        m.g_kv = sb("g_kv", [P, KT])
        m.bank = [c.enter_context(nc.psum_tensor(f"bank{i}", [P, 512], F32)) for i in range(8)]
        m.spill = nc.dram_tensor("h_spill", [KT, P, T], F32, kind="Internal").ap()
        used, done = [0], []

        def phase(f, *args):
            used[0] += 1
            with ExitStack() as stack:
                own = Own(nc, stack, used[0])
                f(nc, m, own, *args)
                done.extend(own.sems)

        with nc.Block() as block:
            @block.scalar
            def _(act):
                act.preload_act_table_set("natural_log_exp_and_others")
        phase(constants)
        phase(embed)
        phase(mixer_a)
        phase(out_and_mlp, d["w_out_a"][0], d["w_up"][0], d["w_down"][0], m.g_mlp[0], True)
        nc.clear_and_free_semaphores(done)
        nc.all_engine_barrier()
        phase(mixer_b)
        phase(out_and_mlp, d["w_out_b"][0], d["w_up"][1], d["w_down"][1], m.g_mlp[1], False)
        phase(final)


def kernel(**inputs):
    import numpy as _np
    import concourse.bacc as _bacc
    from concourse.bass_utils import run_bass_kernel_spmd as _run

    nc = _bacc.Bacc("TRN2", target_bir_lowering=False, num_devices=1)
    arrays, d = {}, {}
    for name in INPUTS:
        a = _np.ascontiguousarray(inputs[name])
        arrays[f"in_{name}"] = a
        d[name] = nc.dram_tensor(f"in_{name}", a.shape, mybir.dt.from_np(a.dtype), kind="ExternalInput").ap()
    for name, shape in OUTPUTS:
        d[name] = nc.dram_tensor(f"out_{name}", shape, F32, kind="ExternalOutput").ap()
    program(nc, d)
    r = _run(nc, [arrays], core_ids=[0])
    return tuple(r.results[0][f"out_{name}"] for name, _ in OUTPUTS)
```
